# Optimizing a Trainium2 kernel written in Bass

```python
import math
import jax, jax.numpy as jnp
from jax import lax
import numpy as np

D_MODEL = 2048
BATCH = 1
SEQ = 256
DEPTH = 2

N_A_LAYERS = DEPTH // 2
N_B_LAYERS = DEPTH - N_A_LAYERS
CONV_WIDTH = 31
CONV_DIM = D_MODEL
HEAD_DIM = 128
N_HEADS = D_MODEL // HEAD_DIM
ATTN_DIM = N_HEADS * HEAD_DIM
DILATED_GROUPS = ((128, 1), (512, 4), (2048, 16))
N_GROUPS = len(DILATED_GROUPS)
BLOCK = 128
N_BUCKETS = 32
MAX_EXACT = N_BUCKETS // 2
MAX_DISTANCE = 2048
EPS = 1e-6

kernel_name = "yoco_conformer_dilated_hybrid"

def rmsnorm(x, g):
    xf = x.astype(jnp.float32)
    y = xf * lax.rsqrt(jnp.mean(xf * xf, axis=-1, keepdims=True) + EPS)
    return (y * g.astype(jnp.float32)).astype(x.dtype)

def t5_bucket(dist):
    large = MAX_EXACT + (jnp.log(jnp.maximum(dist, 1).astype(jnp.float32) / MAX_EXACT)
                         / math.log(MAX_DISTANCE / MAX_EXACT)
                         * (N_BUCKETS - MAX_EXACT)).astype(jnp.int32)
    large = jnp.minimum(large, N_BUCKETS - 1)
    return jnp.where(dist < MAX_EXACT, dist, large)

def conformer_mixer(h, w_in, conv_w, conv_b, ln_g, ln_b, w_out):
    proj = jnp.einsum('bsd,de->bse', h, w_in)
    a, b, z = jnp.split(proj, 3, axis=-1)
    u = a * jax.nn.sigmoid(b)
    c = lax.conv_general_dilated(u, conv_w[:, None, :].astype(u.dtype), (1,),
                                 [(CONV_WIDTH - 1, 0)],
                                 dimension_numbers=('NWC', 'WIO', 'NWC'),
                                 feature_group_count=CONV_DIM) + conv_b
    cf = c.astype(jnp.float32)
    mu = jnp.mean(cf, axis=-1, keepdims=True)
    var = jnp.mean(jnp.square(cf - mu), axis=-1, keepdims=True)
    cn = (cf - mu) * lax.rsqrt(var + EPS) * ln_g.astype(jnp.float32) + ln_b.astype(jnp.float32)
    y = jax.nn.silu(cn).astype(h.dtype) * jax.nn.silu(z)
    return jnp.einsum('bse,ed->bsd', y, w_out)

def dilated_branch(q, k, v, window, dil, rel_bias):
    B, S, H, Dh = q.shape
    L = S // dil
    w_sub = window // dil
    nb = -(-L // BLOCK)
    Lp = nb * BLOCK
    N = B * dil

    def to_blocks(t):
        t = t.reshape(B, L, dil, H, Dh).transpose(0, 2, 1, 3, 4).reshape(N, L, H, Dh)
        t = jnp.pad(t, ((0, 0), (0, Lp - L), (0, 0), (0, 0)))
        return t.reshape(N, nb, BLOCK, H, Dh)

    def with_prev(t):
        prev = jnp.pad(t[:, :-1], ((0, 0), (1, 0), (0, 0), (0, 0), (0, 0)))
        return jnp.concatenate([prev, t], axis=2)

    qb = to_blocks(q).astype(jnp.float32)
    kk = with_prev(to_blocks(k)).astype(jnp.float32)
    vv = with_prev(to_blocks(v)).astype(jnp.float32)

    delta = (jnp.arange(BLOCK)[:, None] + BLOCK) - jnp.arange(2 * BLOCK)[None, :]
    local = (delta >= 0) & (delta <= w_sub)
    key_pos = jnp.arange(nb)[:, None] * BLOCK - BLOCK + jnp.arange(2 * BLOCK)[None, :]
    mask = local[None] & (key_pos >= 0)[:, None, :]
    bias = rel_bias[t5_bucket(jnp.clip(delta, 0) * dil)]
    bias = bias.astype(jnp.float32).transpose(2, 0, 1)

    s = jnp.einsum('nbqhd,nbkhd->nbhqk', qb, kk) * (HEAD_DIM ** -0.5) + bias
    s = jnp.where(mask[None, :, None], s, -jnp.inf)
    m = jnp.max(s, axis=-1, keepdims=True)
    p = jnp.exp(s - m)
    den = jnp.sum(p, axis=-1, keepdims=True)
    o = jnp.einsum('nbhqk,nbkhd->nbqhd', p, vv) / den.transpose(0, 1, 3, 2, 4)
    lse = (m + jnp.log(den))[..., 0].transpose(0, 1, 3, 2)

    def from_blocks(t):
        rest = t.shape[3:]
        t = t.reshape(N, Lp, *rest)[:, :L].reshape(B, dil, L, *rest)
        return jnp.swapaxes(t, 1, 2).reshape(B, S, *rest)

    return from_blocks(o), from_blocks(lse)

def shared_kv(x, kv_norm, w_kv):
    B, S, _ = x.shape
    kv = jnp.einsum('bsd,de->bse', rmsnorm(x, kv_norm), w_kv)
    parts = jnp.split(kv, 2 * N_GROUPS, axis=-1)
    return [(parts[2 * g].reshape(B, S, N_HEADS, HEAD_DIM),
             parts[2 * g + 1].reshape(B, S, N_HEADS, HEAD_DIM)) for g in range(N_GROUPS)]

def dilated_mixer(h, w_in, w_out, kv, rel_bias):
    B, S, _ = h.shape
    parts = jnp.split(jnp.einsum('bsd,de->bse', h, w_in), N_GROUPS + 1, axis=-1)
    outs, lses = [], []
    for g, (window, dil) in enumerate(DILATED_GROUPS):
        q = parts[g].reshape(B, S, N_HEADS, HEAD_DIM)
        o, lse = dilated_branch(q, kv[g][0], kv[g][1], window, dil, rel_bias)
        outs.append(o)
        lses.append(lse)
    alpha = jax.nn.softmax(jnp.stack(lses), axis=0)
    o = jnp.sum(alpha[..., None] * jnp.stack(outs), axis=0).reshape(B, S, ATTN_DIM)
    y = o.astype(h.dtype) * jax.nn.silu(parts[-1])
    return jnp.einsum('bse,ed->bsd', y, w_out)

def setup_inputs(seed: int = 0) -> dict:
    key = jax.random.key(seed)
    ks = jax.random.split(key, 16)
    f32 = jnp.float32
    D, E = D_MODEL, CONV_DIM
    nrm = lambda k, shape, scale: jax.random.normal(k, shape, f32) * scale
    return {
        "x": nrm(ks[0], (BATCH, SEQ, D), 1.0),
        "a_norm": 1.0 + nrm(ks[1], (N_A_LAYERS, D), 0.02),
        "a_w_in": nrm(ks[2], (N_A_LAYERS, D, 3 * E), D ** -0.5),
        "a_conv_w": nrm(ks[3], (N_A_LAYERS, CONV_WIDTH, E), CONV_WIDTH ** -0.5),
        "a_conv_b": nrm(ks[4], (N_A_LAYERS, E), 0.02),
        "a_ln_g": 1.0 + nrm(ks[5], (N_A_LAYERS, E), 0.02),
        "a_ln_b": nrm(ks[6], (N_A_LAYERS, E), 0.02),
        "a_w_out": nrm(ks[7], (N_A_LAYERS, E, D), E ** -0.5),
        "kv_norm": 1.0 + nrm(ks[8], (D,), 0.02),
        "w_kv": nrm(ks[9], (D, 2 * N_GROUPS * ATTN_DIM), D ** -0.5),
        "b_norm": 1.0 + nrm(ks[10], (N_B_LAYERS, D), 0.02),
        "b_w_in": nrm(ks[11], (N_B_LAYERS, D, (N_GROUPS + 1) * ATTN_DIM), D ** -0.5),
        "b_w_out": nrm(ks[12], (N_B_LAYERS, ATTN_DIM, D), ATTN_DIM ** -0.5),
        "rel_bias": nrm(ks[13], (N_BUCKETS, N_HEADS), 0.2),
        "final_norm": 1.0 + nrm(ks[14], (D,), 0.02),
    }

def reference(x, a_norm, a_w_in, a_conv_w, a_conv_b, a_ln_g, a_ln_b, a_w_out,
              kv_norm, w_kv, b_norm, b_w_in, b_w_out, rel_bias, final_norm):
    kv = None
    for layer in range(DEPTH):
        if layer < N_A_LAYERS:
            i = layer
            x = x + conformer_mixer(rmsnorm(x, a_norm[i]), a_w_in[i], a_conv_w[i], a_conv_b[i],
                                    a_ln_g[i], a_ln_b[i], a_w_out[i])
        else:
            if kv is None:
                kv = shared_kv(x, kv_norm, w_kv)
            j = layer - N_A_LAYERS
            x = x + dilated_mixer(rmsnorm(x, b_norm[j]), b_w_in[j], b_w_out[j], kv, rel_bias)
    return rmsnorm(x, final_norm)


_drawn_inputs = setup_inputs


def setup_inputs(seed=0):
    import zlib

    import numpy as np

    out = dict(_drawn_inputs(seed))
    spreads = {}
    factors = {'a_norm': 5.271,
     'a_conv_b': 3.67,
     'a_ln_g': 6.616,
     'a_ln_b': 7.917,
     'kv_norm': 8.0,
     'b_norm': 8.0,
     'rel_bias': 3.376,
     'final_norm': 2.785}
    for name, (base, spread) in spreads.items():
        noise = np.random.default_rng([zlib.crc32(name.encode()), seed]).standard_normal(out[name].shape)
        drawn = base * np.exp(spread * noise) if base else spread * noise
        out[name] = __import__('jax').numpy.asarray(drawn.astype(out[name].dtype))
    for name, factor in factors.items():
        out[name] = (out[name] * factor).astype(out[name].dtype)
    return out
```

```python
import math
from contextlib import ExitStack

import concourse.bass as bass
from concourse import mybir
import numpy as np

F32 = mybir.dt.float32
F32R = mybir.dt.float32r
ALU = mybir.AluOpType
ACT = mybir.ActivationFunctionType
AX = mybir.AxisListType

P = 128
S = 256
D = 2048
KT = D // P
TT = S // P
HEADS = D // P
GROUPS = ((128, 1), (512, 4), (2048, 16))
NG = len(GROUPS)
TAPS = 31
BUCKETS = 32
MAX_DISTANCE = 2048
EPS = 1e-6
MASKED = -1e30
SCALE = float(P) ** -0.5
SLAB = 2048
HALF = SLAB // 2
CHUNK = 512
CHUNKS = D // CHUNK
RKT = 4
BIAS_W = 2 * S
ROW_CONV_B, ROW_LN_G, ROW_LN_B, ROW_A_NORM, ROW_KV_NORM, ROW_B_NORM = range(TAPS, TAPS + 6)
ROWS = TAPS + 6


class Stream:

    def __init__(self, base, count, per_turn, ring, half_ring, lo_base):
        self.base, self.count, self.per_turn = base, count, per_turn
        self.ring, self.half_ring, self.lo_base = ring, half_ring, lo_base

    def slot(self, j):
        return RAW_SLOTS - self.ring + j % self.ring

    def half_slot(self, half):
        return HALF_SLOTS - self.half_ring + half % self.half_ring

    def slabs_before(self, turn):
        return self.base + turn * self.per_turn

    def mm_halves(self, turn, half):
        return 2 * self.base + turn * (2 * self.per_turn) + (half + 1)

    def lo_halves(self, turn, half):
        return self.lo_base + turn * (2 * self.per_turn) + (half + 1)


RAW_SLOTS, HALF_SLOTS = 5, 6
CONV = Stream(0, 3 * KT, 3, 3, 6, 0)
A_OUT = Stream(3 * KT, CHUNKS * KT // RKT, KT // RKT, 4, 4, 6 * KT)
QKV = Stream(A_OUT.base + A_OUT.count, HEADS * (3 * NG + 1), 3 * NG + 1, 5, 5, 0)
B_OUT = Stream(QKV.base + QKV.count, A_OUT.count, A_OUT.per_turn, 4, 4, A_OUT.lo_base + 2 * A_OUT.count)


def fills(stream, slot):
    n = 0
    for s in (CONV, A_OUT, QKV, B_OUT):
        if s is stream:
            return n
        if slot >= RAW_SLOTS - s.ring:
            n += s.count // s.ring


def positive(eng, sem, value):
    if not isinstance(value, int) or value > 0:
        eng.wait_ge(sem, value)


def build(nc, x, a_norm, a_w_in, a_conv_w, a_conv_b, a_ln_g, a_ln_b, a_w_out, kv_norm, w_kv, b_norm,
          b_w_in, b_w_out, rel_bias, final_norm, bucket_rows, out):
    ctx = ExitStack()
    with ctx:
        def sb(name, shape, dt=F32):
            return ctx.enter_context(nc.sbuf_tensor(name, shape, dt))

        def shared(*tensors):
            with ExitStack() as early:
                return [early.enter_context(nc.sbuf_tensor(n, s, d)) for n, s, d in tensors]

        def sem(name):
            return ctx.enter_context(nc.semaphore(name))

        raw = sb("raw", [P, RAW_SLOTS, SLAB])
        w_hi = sb("w_hi", [P, HALF_SLOTS, HALF], F32R)
        w_lo = sb("w_lo", [P, HALF_SLOTS, HALF], F32R)
        ident = sb("ident", [P, P])
        mean_w = sb("mean_w", [P, P])
        param = sb("param", [P, KT, ROWS])
        taps = sb("taps", [P, TAPS + 1])
        stat = sb("stat", [P, 32])

        act_a = sb("act_a", [P, KT, 2, S], F32R)
        conv, gate = shared(("conv", [P, KT, S], F32), ("gate", [P, KT, S], F32))
        (param_rows,) = shared(("param_rows", [ROWS, D], F32))
        resid, gain_row = shared(("resid", [P, TT, D], F32), ("gain_row", [P, D], F32))
        act_b = sb("act_b", [P, KT, 2, S], F32R)
        (x_sb,) = shared(("x_sb", [P, TT, D], F32))
        y2 = sb("y2", [P, KT, S])
        upper = sb("upper", [P, 3, S])
        xn, u, a_sum, b_sum, b_sig, z_sum, z_sig, odd_taps, ln_std, ln_rstd = shared(
            ("xn", [P, TT, D], F32), ("u", [P, TAPS - 1 + S], F32), ("a_sum", [P, S], F32),
            ("b_sum", [P, S], F32), ("b_sig", [P, S], F32), ("z_sum", [P, S], F32),
            ("z_sig", [P, S], F32), ("odd_taps", [P, S], F32), ("ln_std", [P, S], F32),
            ("ln_rstd", [P, S], F32))
        squares = xn[:, :, :].rearrange("p t (b k s) -> p (t b) k s", b=2, s=S)
        q_t = sb("q_t", [P, NG, S])
        k_t = sb("k_t", [P, NG, S])
        v_t = sb("v_t", [P, NG, S])
        v_rows = sb("v_rows", [P, NG, TT, P])
        prob = sb("prob", [P, NG * 3 * P])
        prob_t = sb("prob_t", [P, NG, 3 * P])
        bias = sb("bias", [P, NG, S])
        z_t = sb("z_t", [P, S])
        z_tanh = sb("z_tanh", [P, S])
        z_gate = sb("z_gate", [P, S])

        bank = [ctx.enter_context(nc.psum_tensor(f"bank{i}", [P, 512], F32)) for i in range(8)]

        rel = raw[0:BUCKETS + 1, 0, NG * BIAS_W:NG * BIAS_W + HEADS]
        buckets = raw[0:BUCKETS + 1, 0, 0:NG * BIAS_W]
        bias_vec = raw[0:HEADS, 1, 0:NG * BIAS_W]

        bias_dram = nc.dram_tensor("bias_dram", [HEADS, NG * BIAS_W], F32, kind="Internal")
        resid_dram = nc.dram_tensor("resid_dram", [P, TT, D], F32, kind="Internal")

        raw_in = [sem(f"raw_in{i}") for i in range(RAW_SLOTS)]
        hi_done, lo_pool, lo_dve, mm_done = sem("hi_done"), sem("lo_pool"), sem("lo_dve"), sem("mm_done")
        x_in = [sem(f"x_in{t}") for t in range(TT)]
        rows_in, bias_in, consts, rel_mask = sem("rows_in"), sem("bias_in"), sem("consts"), sem("rel_mask")
        x_squared, std_ready, rstd_ready = sem("x_squared"), sem("std_ready"), sem("rstd_ready")
        x_normed, x_turned = sem("x_normed"), sem("x_turned")
        rows_turned, param_ready = sem("rows_turned"), sem("param_ready")
        vec_made, vec_copied, vec_stored = sem("vec_made"), sem("vec_copied"), sem("vec_stored")
        in_hi, in_lo = sem("in_hi"), sem("in_lo")
        eps_set = sem("eps_set")
        upper_copied, summed = sem("upper_copied"), sem("summed")
        b_gated, z_gated, gate_ready = sem("b_gated"), sem("z_gated"), sem("gate_ready")
        u_ready, taps_copied, tap_done = sem("u_ready"), sem("taps_copied"), sem("tap_done")
        mean_ready, centered, squared, var_part = sem("mean_ready"), sem("centered"), sem("squared"), sem("var_part")
        ln_std_ready, ln_rstd_ready = sem("ln_std_ready"), sem("ln_rstd_ready")
        ln_scaled, swished, y_ready, y_hi, y_lo = (
            sem("ln_scaled"), sem("swished"), sem("y_ready"), sem("y_hi"), sem("y_lo"))
        x1_added, x1_squared, x1_summed, resid_stored = (
            sem("x1_added"), sem("x1_squared"), sem("x1_summed"), sem("resid_stored"))
        x1_std, x1_rstd, x1_normed, x1_turned = sem("x1_std"), sem("x1_rstd"), sem("x1_normed"), sem("x1_turned")
        kv_hi, kv_lo, qb_hi, qb_lo = sem("kv_hi"), sem("kv_lo"), sem("qb_hi"), sem("qb_lo")
        bias_loaded, bias_added, max_ready, exp_done = (
            sem("bias_loaded"), sem("bias_added"), sem("max_ready"), sem("exp_done"))
        scores_done, v_turned, v_copied = sem("scores_done"), sem("v_turned"), sem("v_copied")
        z_tanh_ready, z_gate_ready = sem("z_tanh_ready"), sem("z_gate_ready")
        row_maxed, rden_ready, prob_ready, prob_turned, prob_copied = (
            sem("row_maxed"), sem("rden_ready"), sem("prob_ready"), sem("prob_turned"), sem("prob_copied"))
        attended, y2_ready, y2_hi, y2_lo = sem("attended"), sem("y2_ready"), sem("y2_hi"), sem("y2_lo")
        resid_in, gain_in = sem("resid_in"), sem("gain_in")
        x2_added, x2_squared, x2_summed, x2_std, x2_rstd = (
            sem("x2_added"), sem("x2_squared"), sem("x2_summed"), sem("x2_std"), sem("x2_rstd"))
        out_ready, out_stored = sem("out_ready"), sem("out_stored")

        sq_sum = stat[:, 0:2]
        std = stat[:, 2:4]
        rstd = stat[:, 4:6]
        sq_part = stat[:, 6:14].rearrange("p (t c) -> p t c", t=TT)
        row_max = stat[:, 14:16]
        neg_max = stat[:, 16:18]
        den = stat[:, 18:20]
        rden = stat[:, 20:22]
        scrap = stat[:, 22:23]

        def load_slab(sp, stream, turn, j, src):
            slot = stream.slot(j)
            if isinstance(turn, int) and turn == 0 and j < stream.ring:
                before = {id(CONV): None, id(A_OUT): CONV, id(QKV): A_OUT, id(B_OUT): QKV}[id(stream)]
                if before is not None:
                    last = 2 * (before.count + j - stream.ring + 1)
                    sp.wait_ge(lo_dve if before is QKV else lo_pool, before.lo_base + last)
            else:
                sp.wait_ge(lo_dve if stream is QKV else lo_pool,
                           stream.lo_halves(turn, 2 * (j - stream.ring) + 1))
            sp.dma_start(raw[:, slot, :], src).then_inc(raw_in[slot], 16)

        def split_hi(act, stream, turn, j):
            slot = stream.slot(j)
            loads = fills(stream, slot) + j // stream.ring + 1
            for half in (2 * j, 2 * j + 1):
                part = (half % 2) * HALF
                if half % 2 == 0:
                    act.wait_ge(raw_in[slot], 16 * (turn * (stream.per_turn // stream.ring) + loads))
                positive(act, mm_done, stream.mm_halves(turn, half - stream.half_ring))
                nc.scalar.activation(w_hi[:, stream.half_slot(half), :], raw[:, slot, part:part + HALF],
                                     ACT.Copy).then_inc(hi_done, 1)

        def split_lo(eng, stream, turn, j, done):
            slot = stream.slot(j)
            for half in (2 * j, 2 * j + 1):
                part = (half % 2) * HALF
                eng.wait_ge(hi_done, stream.mm_halves(turn, half))
                eng.tensor_tensor(w_lo[:, stream.half_slot(half), :], raw[:, slot, part:part + HALF],
                                  w_hi[:, stream.half_slot(half), :].bitcast(F32),
                                  ALU.subtract).then_inc(done, 1)

        def project(pe, stream, turn, j, dst, source, source_ready=None):
            for half in (2 * j, 2 * j + 1):
                slot = stream.half_slot(half)
                pe.wait_ge(lo_dve if stream is QKV else lo_pool, stream.lo_halves(turn, half))
                for k in range(KT // 2):
                    kt = (half % 2) * (KT // 2) + k
                    if source_ready is not None:
                        pe.wait_ge(source_ready, kt + 1)
                    nc.tensor.matmul(dst[:, 0:2 * S], w_hi[:, slot, k * P:(k + 1) * P],
                                     source[:, kt, :, :], start=(kt == 0), stop=False)
                    mm = nc.tensor.matmul(dst[:, 0:S], w_lo[:, slot, k * P:(k + 1) * P],
                                          source[:, kt, 0, :], start=False, stop=(kt == KT - 1))
                mm.then_inc(mm_done, 1)

        def out_project(pe, stream, c, q, banks, source, ready):
            for half in (2 * q, 2 * q + 1):
                slot = stream.half_slot(half)
                pe.wait_ge(lo_pool, stream.lo_halves(c, half))
                for k in range(RKT // 2):
                    kt = half * (RKT // 2) + k
                    if ready is not None:
                        pe.wait_ge(ready, kt + 1)
                    wide_hi = w_hi[:, slot, k * CHUNK:(k + 1) * CHUNK]
                    wide_lo = w_lo[:, slot, k * CHUNK:(k + 1) * CHUNK]
                    for t in range(TT):
                        y_h, y_l = (source[:, kt, part, t * P:(t + 1) * P] for part in (0, 1))
                        nc.tensor.matmul(banks[t][:, :], y_h, wide_hi, start=(kt == 0), stop=False)
                        nc.tensor.matmul(banks[t][:, :], y_h, wide_lo, start=False, stop=False)
                        mm = nc.tensor.matmul(banks[t][:, :], y_l, wide_hi, start=False, stop=(kt == KT - 1))
                mm.then_inc(mm_done, 1)

        w_in_cols = a_w_in[0].rearrange("(kt p) n -> p kt n", p=P)
        kv_cols = w_kv.rearrange("(kt p) n -> p kt n", p=P)
        q_cols = b_w_in[0].rearrange("(kt p) n -> p kt n", p=P)

        def out_slab(w, c, q):
            return w.rearrange("(kt p) n -> p kt n", p=P)[:, q * RKT:(q + 1) * RKT, c * CHUNK:(c + 1) * CHUNK]

        def head_slab(j, first_col):
            if j < 2 * NG:
                v, g = divmod(j, NG)
                return kv_cols[:, :, bass.ds(first_col + (2 * g + v) * D, P)]
            return q_cols[:, :, bass.ds(first_col + (j - 2 * NG) * D, P)]

        block = ctx.enter_context(nc.Block())

        @block.sync
        def _(sp):
            x_rows = x.rearrange("b (t p) d -> p (b t) d", p=P)
            for t in range(TT):
                sp.dma_start(x_sb[:, t, :], x_rows[:, t, :]).then_inc(x_in[t], 16)
            for j in range(3):
                load_slab(sp, CONV, 0, j, w_in_cols[:, :, j * D:j * D + P])
            with sp.Fori(1, KT) as c:
                cols = [sp.snap(c * P + j * D) for j in range(3)]
                for j in range(3):
                    load_slab(sp, CONV, c, j, w_in_cols[:, :, bass.ds(cols[j], P)])
            sp.wait_ge(vec_copied, NG)
            sp.dma_start(bias_dram.ap(), bias_vec).then_inc(vec_stored, 16)
            sp.wait_ge(vec_stored, 16)
            for c in range(CHUNKS):
                for q in range(A_OUT.per_turn):
                    load_slab(sp, A_OUT, c, q, out_slab(a_w_out[0], c, q))

            def load_bias(first):
                src = bass.AP(bias_dram, first, [[1, P], [BIAS_W, NG], [1, S]])
                sp.dma_start(bias[:, :, :], src).then_inc(bias_loaded, 16)

            for j in range(QKV.per_turn):
                load_slab(sp, QKV, 0, j, head_slab(j, 0))
                if j == 1:
                    sp.wait_ge(x1_turned, TT * KT)
                    sp.dma_start(resid_dram.ap(), x_sb[:, :, :]).then_inc(resid_stored, 16)
            load_bias(P)
            with sp.Fori(1, HEADS) as h:
                col = sp.snap(h * P)
                cols = [sp.snap(col + (2 * (j % NG) + j // NG) * D) if j < 2 * NG
                        else sp.snap(col + (j - 2 * NG) * D) for j in range(QKV.per_turn)]
                first = sp.snap(h * (NG * BIAS_W) + P)
                for j in range(QKV.per_turn):
                    w = kv_cols if j < 2 * NG else q_cols
                    load_slab(sp, QKV, h, j, w[:, :, bass.ds(cols[j], P)])
                sp.wait_ge(bias_added, 3 * h)
                load_bias(first)
            for c in range(CHUNKS):
                for q in range(B_OUT.per_turn):
                    load_slab(sp, B_OUT, c, q, out_slab(b_w_out[0], c, q))
                    if (c, q) == (0, 1):
                        sp.wait_ge(mm_done, QKV.mm_halves(HEADS - 1, 2 * QKV.per_turn - 1))
                        sp.wait_ge(resid_stored, 16)
                        sp.dma_start(resid[:, :, :], resid_dram.ap()).then_inc(resid_in, 16)
                        sp.dma_start(gain_row[:, :], final_norm.rearrange("(a n) -> a n", a=1)
                                     .partition_broadcast(P)[:, 0, :]).then_inc(gain_in, 16)
            out_rows = out.rearrange("b (t p) d -> p (b t) d", p=P)
            for t in range(TT):
                sp.wait_ge(out_ready, t + 1)
                sp.dma_start(out_rows[:, t, :], resid[:, t, :]).then_inc(out_stored, 16)
            sp.wait_ge(out_stored, 16 * TT)

        @block.gpsimd
        def _(pool):
            nc.gpsimd.memset(raw[BUCKETS:BUCKETS + 1, 0, NG * BIAS_W:NG * BIAS_W + HEADS],
                             MASKED).then_inc(rel_mask, 1)
            pool.wait_ge(rel_mask, 1)
            nc.gpsimd.memset(ident[:, :], 0.0).then_inc(consts, 1)
            nc.gpsimd.memset(mean_w[:, :], 1.0 / D).then_inc(consts, 1)
            pool.wait_ge(consts, 2)
            nc.gpsimd.affine_select(out=ident[:, :], in_=ident[:, :], compare_op=ALU.not_equal, fill=1.0,
                                    base=0, pattern=[[-1, P]], channel_multiplier=1).then_inc(consts, 1)
            with pool.Fori(0, KT) as c:
                for j in range(3):
                    split_lo(pool, CONV, c, j, lo_pool)
            with pool.Fori(0, CHUNKS) as c:
                for q in range(A_OUT.per_turn):
                    split_lo(pool, A_OUT, c, q, lo_pool)
            with pool.Fori(0, CHUNKS) as c:
                for q in range(B_OUT.per_turn):
                    split_lo(pool, B_OUT, c, q, lo_pool)

        @block.scalar
        def _(act):
            for first, src in ((0, a_conv_w[0]), (ROW_CONV_B, a_conv_b), (ROW_LN_G, a_ln_g),
                               (ROW_LN_B, a_ln_b), (ROW_A_NORM, a_norm),
                               (ROW_KV_NORM, kv_norm.rearrange("(a n) -> a n", a=1)), (ROW_B_NORM, b_norm)):
                act.dma_start(param_rows[first:first + src.shape[0], :], src).then_inc(rows_in, 16)
            act.dma_start(buckets, bucket_rows).then_inc(bias_in, 16)
            act.dma_start(rel[0:BUCKETS, :], rel_bias).then_inc(bias_in, 16)

            for t in range(TT):
                act.wait_ge(x_in[t], 16)
                nc.scalar.activation(xn[:, t, :], x_sb[:, t, :], ACT.Square,
                                     accum_out=sq_sum[:, t:t + 1]).then_inc(x_squared, 1)
            act.wait_ge(x_squared, TT)
            act.wait_ge(eps_set, 2)
            nc.scalar.activation(std, sq_sum, ACT.Sqrt, bias=stat[:, 23:24], scale=1.0 / D).then_inc(std_ready, 1)
            act.wait_ge(std_ready, 1)
            nc.scalar.activation(scrap, std[:, 0:1], ACT.Sigmoid).then_inc(std_ready, 1)
            split_hi(act, CONV, 0, 0)
            split_hi(act, CONV, 0, 1)
            act.wait_ge(param_ready, 2)
            for kt in range(KT):
                act.wait_ge(x_turned, 2 * TT * (kt // 2 + 1))
                nc.scalar.activation(act_a[:, kt, 0, :], bank[kt // 2][:, (kt % 2) * S:(kt % 2 + 1) * S],
                                     ACT.Copy, scale=param[:, kt, ROW_A_NORM:ROW_A_NORM + 1]).then_inc(in_hi, 1)

            def copy_upper(c, j):
                act.wait_ge(mm_done, CONV.mm_halves(c, 2 * j + 1))
                if j == 0:
                    positive(act, summed, 3 * c - 2)
                else:
                    act.wait_ge(summed, 3 * c + 1)
                nc.scalar.activation(upper[:, j, :], bank[j][:, S:2 * S], ACT.Copy).then_inc(upper_copied, 1)

            def gate_b(c):
                act.wait_ge(summed, 3 * c + 2)
                nc.scalar.activation(b_sig[:, :], b_sum[:, :], ACT.Sigmoid).then_inc(b_gated, 1)

            def gate_z(c):
                act.wait_ge(summed, 3 * c + 3)
                nc.scalar.activation(z_sig[:, :], z_sum[:, :], ACT.Sigmoid).then_inc(z_gated, 1)

            split_hi(act, CONV, 0, 2)
            copy_upper(0, 0)
            with act.Fori(1, KT) as c:
                split_hi(act, CONV, c, 0)
                copy_upper(c - 1, 1)
                split_hi(act, CONV, c, 1)
                gate_b(c - 1)
                copy_upper(c - 1, 2)
                split_hi(act, CONV, c, 2)
                gate_z(c - 1)
                copy_upper(c, 0)
            split_hi(act, A_OUT, 0, 0)
            copy_upper(KT - 1, 1)
            gate_b(KT - 1)
            split_hi(act, A_OUT, 0, 1)
            copy_upper(KT - 1, 2)
            gate_z(KT - 1)

            for q in range(4):
                act.wait_ge(centered, q + 1)
                nc.scalar.activation(squares[:, q, :, :], conv[:, 4 * q:4 * q + 4, :],
                                     ACT.Square).then_inc(squared, 1)
            act.wait_ge(var_part, 4)
            nc.scalar.activation(ln_std[:, :], bank[5][:, 0:S], ACT.Sqrt,
                                 bias=stat[:, 23:24]).then_inc(ln_std_ready, 1)
            for kt in range(KT + 1):
                if kt < KT:
                    act.wait_ge(ln_scaled, kt + 1)
                    nc.scalar.activation(conv[:, kt, :], conv[:, kt, :], ACT.Silu,
                                         bias=param[:, kt, ROW_LN_B:ROW_LN_B + 1],
                                         scale=param[:, kt, ROW_LN_G:ROW_LN_G + 1]).then_inc(swished, 1)
                if kt > 0:
                    act.wait_ge(y_ready, kt)
                    nc.scalar.activation(act_a[:, kt - 1, 0, :], conv[:, kt - 1, :], ACT.Copy).then_inc(y_hi, 1)

            def square_chunk(buf, c, added, done):
                for t in range(TT):
                    act.wait_ge(added, TT * c + t + 1)
                    nc.scalar.activation(xn[:, t, c * CHUNK:(c + 1) * CHUNK], buf[:, t, c * CHUNK:(c + 1) * CHUNK],
                                         ACT.Square, accum_out=sq_part[:, t, c:c + 1]).then_inc(done, 1)

            for n in range(2, A_OUT.count):
                c, q = divmod(n, A_OUT.per_turn)
                split_hi(act, A_OUT, c, q)
                if q == 2 and c > 0:
                    square_chunk(x_sb, c - 1, x1_added, x1_squared)
            split_hi(act, QKV, 0, 0)
            split_hi(act, QKV, 0, 1)
            square_chunk(x_sb, CHUNKS - 1, x1_added, x1_squared)

            act.wait_ge(x1_summed, 1)
            nc.scalar.activation(std, sq_sum, ACT.Sqrt, bias=stat[:, 23:24], scale=1.0 / D).then_inc(x1_std, 1)
            act.wait_ge(x1_std, 1)
            nc.scalar.activation(scrap, std[:, 0:1], ACT.Exp, scale=0.0).then_inc(x1_std, 1)
            for kt in range(KT):
                act.wait_ge(x1_turned, 2 * TT * (kt // 2 + 1))
                nc.scalar.activation(act_a[:, kt, 0, ::-1], bank[kt // 2][:, (kt % 2) * S:(kt % 2 + 1) * S],
                                     ACT.Copy, scale=param[:, kt, ROW_KV_NORM:ROW_KV_NORM + 1]).then_inc(kv_hi, 1)
            for kt in range(KT):
                act.wait_ge(kv_lo, 2 * (kt // 2 + 1))
                nc.scalar.activation(act_b[:, kt, 0, :], bank[kt // 2][:, (kt % 2) * S:(kt % 2 + 1) * S],
                                     ACT.Copy, scale=param[:, kt, ROW_B_NORM:ROW_B_NORM + 1]).then_inc(qb_hi, 1)

            def copy_upper_head(h, j):
                act.wait_ge(mm_done, QKV.mm_halves(h, 2 * j + 1))
                positive(act, summed, 3 * KT + h * QKV.per_turn + (j - 1))
                nc.scalar.activation(upper[:, j % 2, :], bank[j % 2][:, S:2 * S], ACT.Copy).then_inc(upper_copied, 1)

            def tanh_gate(h):
                act.wait_ge(summed, 3 * KT + (h + 1) * QKV.per_turn)
                nc.scalar.activation(z_tanh[:, :], z_t[:, :], ACT.Tanh, scale=0.5).then_inc(z_tanh_ready, 1)

            def copy_v(h):
                act.wait_ge(v_turned, h + 1)
                for b, (g0, n) in enumerate(((0, 2), (2, 1))):
                    nc.scalar.activation(v_rows[:, g0:g0 + n, :, :].rearrange("p g t d -> p (g t d)"),
                                         bank[5 + b][:, 0:n * S], ACT.Copy).then_inc(v_copied, 1)

            def exps(h):
                act.wait_ge(max_ready, h + 1)
                nc.scalar.activation(prob[:, 0:NG * P], prob[:, 0:NG * P], ACT.Exp, bias=neg_max[:, 0:1],
                                     accum_out=den[:, 0:1]).then_inc(exp_done, 1)
                nc.scalar.activation(prob[:, NG * P:], prob[:, NG * P:], ACT.Exp, bias=neg_max[:, 1:2],
                                     accum_out=den[:, 1:2]).then_inc(exp_done, 1)

            def copy_probs(h):
                act.wait_ge(prob_turned, h + 1)
                for g in range(NG):
                    nc.scalar.activation(prob_t[:, g, :], bank[2 + g][:, 0:3 * P], ACT.Copy).then_inc(prob_copied, 1)

            for j in range(2, QKV.per_turn):
                split_hi(act, QKV, 0, j)
                copy_upper_head(0, j - 2)
            with act.Fori(1, HEADS) as h:
                for j in range(QKV.per_turn):
                    split_hi(act, QKV, h, j)
                    if j < 2:
                        copy_upper_head(h - 1, j + QKV.per_turn - 2)
                    else:
                        copy_upper_head(h, j - 2)
                    if j == 2:
                        copy_v(h - 1)
                        tanh_gate(h - 1)
                    if j == 3:
                        exps(h - 1)
                    if j == 6:
                        copy_probs(h - 1)
            last = HEADS - 1
            split_hi(act, B_OUT, 0, 0)
            copy_upper_head(last, QKV.per_turn - 2)
            split_hi(act, B_OUT, 0, 1)
            copy_upper_head(last, QKV.per_turn - 1)
            act.wait_ge(y2_ready, last)
            for kt in range(last):
                nc.scalar.activation(act_a[:, kt, 0, :], y2[:, kt, :], ACT.Copy).then_inc(y2_hi, 1)
            copy_v(last)
            tanh_gate(last)
            exps(last)
            split_hi(act, B_OUT, 0, 2)
            copy_probs(last)
            split_hi(act, B_OUT, 0, 3)
            act.wait_ge(y2_ready, HEADS)
            nc.scalar.activation(act_a[:, last, 0, :], y2[:, last, :], ACT.Copy).then_inc(y2_hi, 1)

            def square_out(c):
                for t in range(TT):
                    act.wait_ge(x2_added, TT * c + t + 1)
                    nc.scalar.activation(y2[:, 8 * t + 2 * c:8 * t + 2 * c + 2, :].rearrange("p k s -> p (k s)"),
                                         resid[:, t, c * CHUNK:(c + 1) * CHUNK], ACT.Square,
                                         accum_out=sq_part[:, t, c:c + 1]).then_inc(x2_squared, 1)

            for n in range(B_OUT.per_turn, B_OUT.count):
                c, q = divmod(n, B_OUT.per_turn)
                split_hi(act, B_OUT, c, q)
                if q == 2 and c > 0:
                    square_out(c - 1)
            square_out(CHUNKS - 1)
            act.wait_ge(x2_summed, 1)
            nc.scalar.activation(std, sq_sum, ACT.Sqrt, bias=stat[:, 23:24], scale=1.0 / D).then_inc(x2_std, 1)

        @block.vector
        def _(dve):
            nc.vector.memset(stat[:, 23:24], EPS).then_inc(eps_set, 1)
            nc.vector.memset(u[:, 0:TAPS - 1], 0.0).then_inc(eps_set, 1)
            dve.wait_ge(std_ready, 1)
            nc.vector.reciprocal(rstd, std).then_inc(rstd_ready, 1)
            dve.wait_ge(rstd_ready, 1)
            for t in range(TT):
                nc.vector.tensor_scalar(xn[:, t, :], x_sb[:, t, :], rstd[:, t:t + 1], None,
                                        ALU.mult).then_inc(x_normed, 1)
            for b in range(2):
                dve.wait_ge(rows_turned, b + 1)
                nc.vector.tensor_copy(param[:, 8 * b:8 * b + 8, :].rearrange("p k r -> p (k r)"),
                                      bank[6 + b][:, 0:8 * ROWS]).then_inc(param_ready, 1)
            for kt in range(KT):
                dve.wait_ge(in_hi, 2 * (kt // 2 + 1))
                if kt == 0:
                    dve.wait_ge(param_ready, 2)
                nc.vector.scalar_tensor_tensor(
                    out=act_a[:, kt, 1, :], in0=bank[kt // 2][:, (kt % 2) * S:(kt % 2 + 1) * S],
                    scalar=param[:, kt, ROW_A_NORM:ROW_A_NORM + 1], in1=act_a[:, kt, 0, :].bitcast(F32),
                    op0=ALU.mult, op1=ALU.subtract).then_inc(in_lo, 1)
            for g in range(NG):
                dve.wait_ge(vec_made, g + 1)
                nc.vector.tensor_copy(bias_vec[:, g * BIAS_W:(g + 1) * BIAS_W], bank[5 + g][0:HEADS, :]
                                      ).then_inc(vec_copied, 1)

            def add_halves(c, j, dst):
                dve.wait_ge(upper_copied, 3 * c + (j + 1))
                nc.vector.tensor_tensor(dst, bank[j][:, 0:S], upper[:, j, :], ALU.add).then_inc(summed, 1)

            def tap(c, k):
                acc = bank[3][:, (k % 2) * S:(k % 2 + 1) * S]
                if k >= 2:
                    dve.wait_ge(tap_done, c * (TAPS + 1) + (k - 1))
                if k == 0:
                    nc.vector.tensor_scalar(acc, u[:, k:k + S], taps[:, k:k + 1], taps[:, TAPS:TAPS + 1],
                                            ALU.mult, ALU.add).then_inc(tap_done, 1)
                elif k == 1:
                    nc.vector.tensor_scalar(acc, u[:, k:k + S], taps[:, k:k + 1], None,
                                            ALU.mult).then_inc(tap_done, 1)
                else:
                    nc.vector.scalar_tensor_tensor(out=odd_taps[:, :] if k == TAPS - 2 else acc,
                                                   in0=u[:, k:k + S], scalar=taps[:, k:k + 1], in1=acc,
                                                   op0=ALU.mult, op1=ALU.add).then_inc(tap_done, 1)

            def join_taps(c, dst):
                dve.wait_ge(tap_done, c * (TAPS + 1) + TAPS)
                nc.vector.tensor_tensor(dst, bank[3][:, 0:S], odd_taps[:, :], ALU.add).then_inc(tap_done, 1)

            def load_taps(c, src):
                dve.wait_ge(u_ready, c + 1)
                nc.vector.tensor_copy(taps[:, :], src).then_inc(taps_copied, 1)
                dve.wait_ge(taps_copied, c + 1)

            def glu(c):
                dve.wait_ge(b_gated, c + 1)
                positive(dve, tap_done, c * (TAPS + 1))
                nc.vector.tensor_tensor(u[:, TAPS - 1:], a_sum[:, :], b_sig[:, :], ALU.mult).then_inc(u_ready, 1)

            def gate_out(c, dst):
                dve.wait_ge(z_gated, c + 1)
                nc.vector.tensor_tensor(dst, z_sum[:, :], z_sig[:, :], ALU.mult).then_inc(gate_ready, 1)

            add_halves(0, 0, a_sum[:, :])
            add_halves(0, 1, b_sum[:, :])
            glu(0)
            add_halves(0, 2, z_sum[:, :])
            with dve.Fori(1, KT) as c:
                tile_before = dve.snap(c - 1)
                dve.wait_ge(u_ready, c)
                add_halves(c, 0, a_sum[:, :])
                gate_out(c - 1, gate[:, bass.ds(tile_before, 1), :].rearrange("p a s -> p (a s)"))
                load_taps(c - 1, param[:, bass.ds(tile_before, 1), 0:TAPS + 1].rearrange("p a r -> p (a r)"))
                for k in range(16):
                    tap(c - 1, k)
                dve.wait_ge(b_gated, c)
                add_halves(c, 1, b_sum[:, :])
                for k in range(16, TAPS):
                    tap(c - 1, k)
                join_taps(c - 1, conv[:, bass.ds(tile_before, 1), :].rearrange("p a s -> p (a s)"))
                glu(c)
                dve.wait_ge(gate_ready, c)
                add_halves(c, 2, z_sum[:, :])
            last = KT - 1
            load_taps(last, param[:, last, 0:TAPS + 1])
            for k in range(TAPS):
                tap(last, k)
            join_taps(last, conv[:, last, :])
            gate_out(last, gate[:, last, :])

            dve.wait_ge(mean_ready, 1)
            for q in range(4):
                mean = bank[4][:, 0:S].unsqueeze(1).to_broadcast([P, 4, S])
                nc.vector.tensor_tensor(conv[:, 4 * q:4 * q + 4, :], conv[:, 4 * q:4 * q + 4, :], mean,
                                        ALU.subtract).then_inc(centered, 1)
            dve.wait_ge(ln_std_ready, 1)
            nc.vector.reciprocal(ln_rstd[:, :], ln_std[:, :]).then_inc(ln_rstd_ready, 1)
            dve.wait_ge(ln_rstd_ready, 1)
            dve.wait_ge(squared, 4)
            dve.wait_ge(gate_ready, KT)
            for kt in range(KT + 2):
                if kt < KT:
                    nc.vector.tensor_tensor(conv[:, kt, :], conv[:, kt, :], ln_rstd[:, :],
                                            ALU.mult).then_inc(ln_scaled, 1)
                if 1 <= kt <= KT:
                    dve.wait_ge(swished, kt)
                    nc.vector.tensor_tensor(conv[:, kt - 1, :], conv[:, kt - 1, :], gate[:, kt - 1, :],
                                            ALU.mult).then_inc(y_ready, 1)
                if kt >= 2:
                    dve.wait_ge(y_hi, kt - 1)
                    nc.vector.tensor_tensor(act_a[:, kt - 2, 1, :], conv[:, kt - 2, :],
                                            act_a[:, kt - 2, 0, :].bitcast(F32), ALU.subtract).then_inc(y_lo, 1)

            for c in range(CHUNKS):
                if c == CHUNKS - 1:
                    split_lo(dve, QKV, 0, 0, lo_dve)
                dve.wait_ge(mm_done, A_OUT.mm_halves(c, 2 * A_OUT.per_turn - 1))
                for t in range(TT):
                    cols = x_sb[:, t, c * CHUNK:(c + 1) * CHUNK]
                    nc.vector.tensor_tensor(cols, bank[2 * (c % 2) + t][:, :], cols, ALU.add).then_inc(x1_added, 1)
            split_lo(dve, QKV, 0, 1, lo_dve)
            dve.wait_ge(x1_squared, TT * CHUNKS)
            nc.vector.tensor_reduce(sq_sum, sq_part, AX.X, ALU.add).then_inc(x1_summed, 1)
            dve.wait_ge(x1_std, 1)
            nc.vector.reciprocal(rstd, std).then_inc(x1_rstd, 1)
            dve.wait_ge(x1_rstd, 1)
            dve.wait_ge(x1_added, TT * CHUNKS)
            for t in range(TT):
                nc.vector.tensor_scalar(xn[:, t, :], x_sb[:, t, :], rstd[:, t:t + 1], None,
                                        ALU.mult).then_inc(x1_normed, 1)
            for kt in range(KT):
                dve.wait_ge(kv_hi, 2 * (kt // 2 + 1))
                nc.vector.scalar_tensor_tensor(
                    out=act_a[:, kt, 1, ::-1], in0=bank[kt // 2][:, (kt % 2) * S:(kt % 2 + 1) * S],
                    scalar=param[:, kt, ROW_KV_NORM:ROW_KV_NORM + 1], in1=act_a[:, kt, 0, ::-1].bitcast(F32),
                    op0=ALU.mult, op1=ALU.subtract).then_inc(kv_lo, 1)
            for kt in range(KT):
                dve.wait_ge(qb_hi, 2 * (kt // 2 + 1))
                nc.vector.scalar_tensor_tensor(
                    out=act_b[:, kt, 1, :], in0=bank[kt // 2][:, (kt % 2) * S:(kt % 2 + 1) * S],
                    scalar=param[:, kt, ROW_B_NORM:ROW_B_NORM + 1], in1=act_b[:, kt, 0, :].bitcast(F32),
                    op0=ALU.mult, op1=ALU.subtract).then_inc(qb_lo, 1)

            def head_sum(h, j):
                dst = [k_t, v_t, q_t][j // NG][:, j % NG, :] if j < 3 * NG else z_t[:, :]
                dve.wait_ge(upper_copied, 3 * KT + h * QKV.per_turn + (j + 1))
                nc.vector.tensor_tensor(dst, bank[j % 2][:, 0:S], upper[:, j % 2, :], ALU.add).then_inc(summed, 1)

            def biased_scores(h):
                dve.wait_ge(scores_done, h + 1)
                dve.wait_ge(bias_loaded, 16 * (h + 1))
                nc.vector.scalar_tensor_tensor(
                    out=prob[:, 0:NG * P].rearrange("p (g k) -> p g k", g=NG),
                    in0=bank[2][:, 0:NG * P].rearrange("p (g k) -> p g k", g=NG), scalar=SCALE,
                    in1=bias[:, :, 0:P], op0=ALU.mult, op1=ALU.add).then_inc(bias_added, 1)
                nc.vector.scalar_tensor_tensor(
                    out=prob[:, NG * P:NG * P + 2 * S].rearrange("p (g k) -> p g k", g=2),
                    in0=bank[3][:, 0:2 * S].rearrange("p (g k) -> p g k", g=2), scalar=SCALE,
                    in1=bias[:, 0:2, :], op0=ALU.mult, op1=ALU.add).then_inc(bias_added, 1)
                nc.vector.scalar_tensor_tensor(
                    out=prob[:, NG * P + 2 * S:], in0=bank[4][:, 0:S], scalar=SCALE,
                    in1=bias[:, 2, :], op0=ALU.mult, op1=ALU.add).then_inc(bias_added, 1)
                for t, cols in enumerate((prob[:, 0:NG * P], prob[:, NG * P:])):
                    dve.wait_ge(bias_added, 3 * h + (1 if t == 0 else 3))
                    nc.vector.tensor_reduce(row_max[:, t:t + 1], cols, AX.X, ALU.max).then_inc(row_maxed, 1)
                dve.wait_ge(row_maxed, 2 * (h + 1))
                nc.vector.tensor_scalar(neg_max, row_max, -1.0, None, ALU.mult).then_inc(max_ready, 1)

            def normalise(h):
                dve.wait_ge(exp_done, 2 * (h + 1))
                nc.vector.reciprocal(rden, den).then_inc(rden_ready, 1)
                dve.wait_ge(rden_ready, h + 1)
                for t, cols in enumerate((prob[:, 0:NG * P], prob[:, NG * P:])):
                    nc.vector.tensor_scalar(cols, cols, rden[:, t:t + 1], None, ALU.mult).then_inc(prob_ready, 1)

            def gated(h, dst):
                dve.wait_ge(z_tanh_ready, h + 1)
                nc.vector.scalar_tensor_tensor(out=z_gate[:, :], in0=z_tanh[:, :], scalar=1.0, in1=z_t[:, :],
                                               op0=ALU.add, op1=ALU.mult).then_inc(z_gate_ready, 1)
                dve.wait_ge(z_gate_ready, h + 1)
                dve.wait_ge(attended, h + 1)
                nc.vector.scalar_tensor_tensor(out=dst, in0=bank[7][:, 0:S], scalar=0.5, in1=z_gate[:, :],
                                               op0=ALU.mult, op1=ALU.mult).then_inc(y2_ready, 1)

            for j in range(2, QKV.per_turn):
                split_lo(dve, QKV, 0, j, lo_dve)
                if j == 2:
                    dve.wait_ge(x1_turned, TT * KT)
                head_sum(0, j - 2)
            with dve.Fori(1, HEADS) as h:
                head_before = dve.snap(h - 1)
                for j in range(QKV.per_turn):
                    split_lo(dve, QKV, h, j, lo_dve)
                    if j < 2:
                        head_sum(h - 1, j + QKV.per_turn - 2)
                    else:
                        if j == 2:
                            dve.wait_ge(scores_done, h)
                        if j == 5:
                            dve.wait_ge(v_turned, h)
                        head_sum(h, j - 2)
                    if j == 2:
                        biased_scores(h - 1)
                    if j == 4:
                        normalise(h - 1)
                    if j == 9:
                        gated(h - 1, y2[:, bass.ds(head_before, 1), :].rearrange("p a s -> p (a s)"))
            last = HEADS - 1
            head_sum(last, QKV.per_turn - 2)
            head_sum(last, QKV.per_turn - 1)
            for kt in range(last):
                dve.wait_ge(y2_hi, kt + 1)
                nc.vector.tensor_tensor(act_a[:, kt, 1, :], y2[:, kt, :], act_a[:, kt, 0, :].bitcast(F32),
                                        ALU.subtract).then_inc(y2_lo, 1)
            biased_scores(last)
            normalise(last)
            gated(last, y2[:, last, :])
            dve.wait_ge(y2_hi, HEADS)
            nc.vector.tensor_tensor(act_a[:, last, 1, :], y2[:, last, :], act_a[:, last, 0, :].bitcast(F32),
                                    ALU.subtract).then_inc(y2_lo, 1)

            dve.wait_ge(resid_in, 16)
            for c in range(CHUNKS):
                dve.wait_ge(mm_done, B_OUT.mm_halves(c, 2 * B_OUT.per_turn - 1))
                for t in range(TT):
                    cols = resid[:, t, c * CHUNK:(c + 1) * CHUNK]
                    nc.vector.tensor_tensor(cols, bank[2 * (c % 2) + t][:, :], cols, ALU.add).then_inc(x2_added, 1)
            dve.wait_ge(x2_squared, TT * CHUNKS)
            nc.vector.tensor_reduce(sq_sum, sq_part, AX.X, ALU.add).then_inc(x2_summed, 1)
            dve.wait_ge(x2_std, 1)
            nc.vector.reciprocal(rstd, std).then_inc(x2_rstd, 1)
            dve.wait_ge(x2_rstd, 1)
            dve.wait_ge(x2_added, TT * CHUNKS)
            dve.wait_ge(gain_in, 16)
            for t in range(TT):
                nc.vector.scalar_tensor_tensor(out=resid[:, t, :], in0=resid[:, t, :], scalar=rstd[:, t:t + 1],
                                               in1=gain_row[:, :], op0=ALU.mult, op1=ALU.mult).then_inc(out_ready, 1)

        @block.tensor
        def _(pe):
            pe.wait_ge(consts, 3)

            pe.wait_ge(rows_in, 7 * 16)
            for b in range(2):
                for k in range(8):
                    kt = 8 * b + k
                    mm = nc.tensor.transpose(bank[6 + b][:, k * ROWS:(k + 1) * ROWS],
                                             param_rows[:, kt * P:(kt + 1) * P], ident[0:ROWS, 0:ROWS])
                mm.then_inc(rows_turned, 1)

            def turn_rows(turned, kt):
                for t in range(TT):
                    nc.tensor.transpose(bank[kt // 2][:, (kt % 2) * S + t * P:(kt % 2) * S + (t + 1) * P],
                                        xn[:, t, kt * P:(kt + 1) * P], ident[:, :]).then_inc(turned, 1)

            pe.wait_ge(x_normed, TT)
            for kt in range(KT):
                if kt == 12:
                    pe.wait_ge(param_ready, 2)
                turn_rows(x_turned, kt)
            pe.wait_ge(bias_in, 32)
            pe.wait_ge(rel_mask, 1)
            pe.wait_ge(in_lo, KT)
            for g in range(NG):
                nc.tensor.matmul(bank[5 + g][0:HEADS, :], rel, buckets[:, g * BIAS_W:(g + 1) * BIAS_W],
                                 start=True, stop=True).then_inc(vec_made, 1)

            for j in range(3):
                project(pe, CONV, 0, j, bank[j], act_a)
            with pe.Fori(1, KT) as c:
                for j in range(3):
                    pe.wait_ge(summed, 3 * c + (j - 2))
                    project(pe, CONV, c, j, bank[j], act_a)

            for kt in range(KT):
                if kt in (0, KT - 1):
                    pe.wait_ge(tap_done, (TAPS + 1) * (KT - 1 if kt == 0 else KT))
                mm = nc.tensor.matmul(bank[4][:, 0:S], mean_w[:, :], conv[:, kt, :], start=(kt == 0),
                                      stop=(kt == KT - 1))
            mm.then_inc(mean_ready, 1)
            for q in range(4):
                pe.wait_ge(squared, q + 1)
                for k in range(4):
                    mm = nc.tensor.matmul(bank[5][:, 0:S], mean_w[:, :], squares[:, q, k, :],
                                          start=(q + k == 0), stop=(q + k == 6))
                mm.then_inc(var_part, 1)

            for c in range(CHUNKS):
                if c >= 2:
                    pe.wait_ge(x1_added, TT * (c - 1))
                for q in range(A_OUT.per_turn):
                    out_project(pe, A_OUT, c, q, bank[2 * (c % 2):2 * (c % 2) + 2], act_a,
                                y_lo if c == 0 else None)

            pe.wait_ge(x1_normed, TT)
            for kt in range(KT):
                turn_rows(x1_turned, kt)

            def scores(h):
                pe.wait_ge(summed, 3 * KT + h * QKV.per_turn + (3 * NG))
                for g in range(NG):
                    nc.tensor.matmul(bank[2][:, g * P:(g + 1) * P], q_t[:, g, 0:P], k_t[:, g, P:2 * P],
                                     start=True, stop=True)
                for g in range(NG):
                    dst = bank[3][:, g * S:(g + 1) * S] if g < 2 else bank[4][:, 0:S]
                    mm = nc.tensor.matmul(dst, q_t[:, g, P:2 * P], k_t[:, g, :], start=True, stop=True)
                mm.then_inc(scores_done, 1)

            def turn_v(h):
                for g in range(NG):
                    for t in range(TT):
                        at = (g % 2) * S + t * P
                        mm = nc.tensor.transpose(bank[5 + g // 2][:, at:at + P], v_t[:, g, t * P:(t + 1) * P],
                                                 ident[:, :])
                mm.then_inc(v_turned, 1)

            def turn_probs(h):
                pe.wait_ge(prob_ready, 2 * (h + 1))
                for g in range(NG):
                    late = NG * P + g * S
                    for n, col in enumerate((g * P, late + P, late)):
                        mm = nc.tensor.transpose(bank[2 + g][:, n * P:(n + 1) * P], prob[:, col:col + P], ident[:, :])
                mm.then_inc(prob_turned, 1)

            def attend(h):
                pe.wait_ge(prob_copied, NG * (h + 1))
                pe.wait_ge(v_copied, 2 * (h + 1))
                for g in range(NG):
                    nc.tensor.matmul(bank[7][:, 0:S], v_rows[:, g, 1, :], prob_t[:, g, 0:S], start=(g == 0), stop=False)
                for g in range(NG):
                    mm = nc.tensor.matmul(bank[7][:, P:S], v_rows[:, g, 0, :], prob_t[:, g, S:S + P],
                                          start=False, stop=(g == NG - 1))
                mm.then_inc(attended, 1)

            def head_slab_product(h, j, ready=None):
                if isinstance(h, int) and h == 0 and j < 2:
                    pe.wait_ge(qb_lo, 2 * (j + 1))
                else:
                    pe.wait_ge(summed, 3 * KT + h * QKV.per_turn + (j - 1))
                project(pe, QKV, h, j, bank[j % 2], act_a if j < 2 * NG else act_b, ready)

            for j in range(QKV.per_turn):
                head_slab_product(0, j, {0: kv_lo, 2 * NG: qb_lo}.get(j))
            with pe.Fori(1, HEADS) as h:
                for j in range(QKV.per_turn):
                    head_slab_product(h, j)
                    if j == 0:
                        scores(h - 1)
                        turn_v(h - 1)
                    if j == 3:
                        turn_probs(h - 1)
                    if j == 6:
                        attend(h - 1)

            last = HEADS - 1
            for c in range(CHUNKS):
                if c >= 2:
                    pe.wait_ge(x2_added, TT * (c - 1))
                if c == 1:
                    pe.wait_ge(prob_copied, NG * HEADS)
                if c == 0:
                    pe.wait_ge(summed, 3 * KT + HEADS * QKV.per_turn)
                    scores(last)
                    turn_v(last)
                for q in range(B_OUT.per_turn):
                    out_project(pe, B_OUT, c, q, bank[2 * (c % 2):2 * (c % 2) + 2], act_a, y2_lo if c == 0 else None)
                    if c == 0 and q == 1:
                        turn_probs(last)
                    if c == 0 and q == 2:
                        attend(last)


INPUTS = ["x", "a_norm", "a_w_in", "a_conv_w", "a_conv_b", "a_ln_g", "a_ln_b", "a_w_out", "kv_norm", "w_kv",
          "b_norm", "b_w_in", "b_w_out", "rel_bias", "final_norm"]


def bucket_table():
    table = np.zeros((BUCKETS + 1, NG, BIAS_W), np.float32)
    exact = BUCKETS // 2
    for g, (window, dil) in enumerate(GROUPS):
        for e in range(BIAS_W):
            dist = e - (S - 1)
            if dist < 0 or dist % dil or dist > window:
                table[BUCKETS, g, e] = 1.0
                continue
            bucket = dist
            if dist >= exact:
                bucket = exact + int(math.log(dist / exact) / math.log(MAX_DISTANCE / exact) * (BUCKETS - exact))
            table[min(bucket, BUCKETS - 1), g, e] = 1.0
    return table.reshape(BUCKETS + 1, NG * BIAS_W)


def kernel(**inputs):
    import concourse.bacc as bacc
    from concourse.bass_utils import run_bass_kernel_spmd

    nc = bacc.Bacc("TRN2", target_bir_lowering=False, num_devices=1)
    arrays = {name: np.ascontiguousarray(inputs[name]) for name in INPUTS}
    arrays["bucket_rows"] = bucket_table()
    args = [nc.dram_tensor(f"{n}_dram", a.shape, mybir.dt.from_np(a.dtype), kind="ExternalInput").ap()
            for n, a in arrays.items()]
    out = nc.dram_tensor("out_dram", (1, S, D), F32, kind="ExternalOutput").ap()
    build(nc, *args, out)
    done = run_bass_kernel_spmd(nc, [{f"{n}_dram": a for n, a in arrays.items()}], core_ids=[0])
    return done.results[0]["out_dram"]
```

```python
import math
from contextlib import ExitStack

import concourse.bass as bass
from concourse import mybir
import numpy as np

F32 = mybir.dt.float32
F32R = mybir.dt.float32r
ALU = mybir.AluOpType
ACT = mybir.ActivationFunctionType
AX = mybir.AxisListType

P = 128
S = 256
D = 2048
KT = D // P
TT = S // P
HEADS = D // P
GROUPS = ((128, 1), (512, 4), (2048, 16))
NG = len(GROUPS)
TAPS = 31
BUCKETS = 32
MAX_DISTANCE = 2048
EPS = 1e-6
MASKED = -1e30
SCALE = float(P) ** -0.5
SLAB = 2048
HALF = SLAB // 2
CHUNK = 512
CHUNKS = D // CHUNK
RKT = 4
BIAS_W = 2 * S
ROW_CONV_B, ROW_LN_G, ROW_LN_B, ROW_A_NORM, ROW_KV_NORM, ROW_B_NORM = range(TAPS, TAPS + 6)
ROWS = TAPS + 6


class Stream:

    def __init__(self, base, count, per_turn, ring, half_ring, lo_base):
        self.base, self.count, self.per_turn = base, count, per_turn
        self.ring, self.half_ring, self.lo_base = ring, half_ring, lo_base

    def slot(self, j):
        return RAW_SLOTS - self.ring + j % self.ring

    def half_slot(self, half):
        return HALF_SLOTS - self.half_ring + half % self.half_ring

    def slabs_before(self, turn):
        return self.base + turn * self.per_turn

    def mm_halves(self, turn, half):
        return 2 * self.base + turn * (2 * self.per_turn) + (half + 1)

    def lo_halves(self, turn, half):
        return self.lo_base + turn * (2 * self.per_turn) + (half + 1)


RAW_SLOTS, HALF_SLOTS = 5, 6
INPUT_ORDER = (("kv", range(0, 4)), ("q", range(0, 2)), ("kv", range(4, KT)), ("q", range(2, 4)))
Y_LOOP_SPLITS = {10: (2, (0,)), 13: (2, (1,))}
LATE_Q_INPUT = {2: range(4, 8), 3: range(8, 12), 4: range(12, KT)}
CONV = Stream(0, 3 * KT, 3, 3, 6, 0)
A_OUT = Stream(3 * KT, CHUNKS * KT // RKT, KT // RKT, 4, 4, 6 * KT)
QKV = Stream(A_OUT.base + A_OUT.count, HEADS * (3 * NG + 1), 3 * NG + 1, 5, 5, 0)
B_OUT = Stream(QKV.base + QKV.count, A_OUT.count, A_OUT.per_turn, 4, 4, A_OUT.lo_base + 2 * A_OUT.count)


def fills(stream, slot):
    n = 0
    for s in (CONV, A_OUT, QKV, B_OUT):
        if s is stream:
            return n
        if slot >= RAW_SLOTS - s.ring:
            n += s.count // s.ring


def positive(eng, sem, value):
    if not isinstance(value, int) or value > 0:
        eng.wait_ge(sem, value)


def build(nc, x, a_norm, a_w_in, a_conv_w, a_conv_b, a_ln_g, a_ln_b, a_w_out, kv_norm, w_kv, b_norm,
          b_w_in, b_w_out, rel_bias, final_norm, bucket_rows, out):
    ctx = ExitStack()
    with ctx:
        def sb(name, shape, dt=F32):
            return ctx.enter_context(nc.sbuf_tensor(name, shape, dt))

        def shared(*tensors):
            with ExitStack() as early:
                return [early.enter_context(nc.sbuf_tensor(n, s, d)) for n, s, d in tensors]

        def sem(name):
            return ctx.enter_context(nc.semaphore(name))

        raw = sb("raw", [P, RAW_SLOTS, SLAB])
        w_hi = sb("w_hi", [P, HALF_SLOTS, HALF], F32R)
        w_lo = sb("w_lo", [P, HALF_SLOTS, HALF], F32R)
        ident = sb("ident", [P, P])
        mean_w = sb("mean_w", [P, P])
        param = sb("param", [P, KT, ROWS])
        taps = sb("taps", [P, TAPS + 1])
        stat = sb("stat", [P, 32])

        act_a = sb("act_a", [P, KT, 2, S], F32R)
        conv, gate = shared(("conv", [P, KT, S], F32), ("gate", [P, KT, S], F32))
        (param_rows,) = shared(("param_rows", [ROWS, D], F32))
        resid, gain_row = shared(("resid", [P, TT, D], F32), ("gain_row", [P, D], F32))
        act_b = sb("act_b", [P, KT, 2, S], F32R)
        (x_sb,) = shared(("x_sb", [P, TT, D], F32))
        y2 = sb("y2", [P, KT, S])
        upper = sb("upper", [P, 3, S])
        xn, u, a_sum, b_sum, b_sig, z_sum, z_sig, odd_taps, ln_std, ln_rstd = shared(
            ("xn", [P, TT, D], F32), ("u", [P, TAPS - 1 + S], F32), ("a_sum", [P, S], F32),
            ("b_sum", [P, S], F32), ("b_sig", [P, S], F32), ("z_sum", [P, S], F32),
            ("z_sig", [P, S], F32), ("odd_taps", [P, S], F32), ("ln_std", [P, S], F32),
            ("ln_rstd", [P, S], F32))
        rows = y2[:, :, :].rearrange("p (t k) s -> p t (k s)", t=TT)
        squares = xn[:, :, :].rearrange("p t (b k s) -> p (t b) k s", b=2, s=S)
        q_t = sb("q_t", [P, NG, S])
        k_t = sb("k_t", [P, NG, S])
        v_t = sb("v_t", [P, NG, S])
        v_rows = sb("v_rows", [P, NG, TT, P])
        prob = sb("prob", [P, NG * 3 * P])
        prob_t = sb("prob_t", [P, NG, 3 * P])
        bias = sb("bias", [P, NG, S])
        z_t = sb("z_t", [P, S])
        z_tanh = sb("z_tanh", [P, S])
        z_gate = sb("z_gate", [P, S])

        bank = [ctx.enter_context(nc.psum_tensor(f"bank{i}", [P, 512], F32)) for i in range(8)]

        rel = raw[0:BUCKETS + 1, 0, NG * BIAS_W:NG * BIAS_W + HEADS]
        buckets = raw[0:BUCKETS + 1, 0, 0:NG * BIAS_W]
        bias_vec = raw[0:HEADS, 1, 0:NG * BIAS_W]

        bias_dram = nc.dram_tensor("bias_dram", [HEADS, NG * BIAS_W], F32, kind="Internal")
        resid_dram = nc.dram_tensor("resid_dram", [P, TT, D], F32, kind="Internal")

        raw_in = [sem(f"raw_in{i}") for i in range(RAW_SLOTS)]
        hi_done, lo_pool, lo_dve, mm_done = sem("hi_done"), sem("lo_pool"), sem("lo_dve"), sem("mm_done")
        x_in = [sem(f"x_in{t}") for t in range(TT)]
        rows_in, bias_in, consts, rel_mask = sem("rows_in"), sem("bias_in"), sem("consts"), sem("rel_mask")
        x_squared, std_ready, rstd_ready = sem("x_squared"), sem("std_ready"), sem("rstd_ready")
        x_normed, x_turned = sem("x_normed"), sem("x_turned")
        rows_turned, param_ready = sem("rows_turned"), sem("param_ready")
        vec_made, vec_copied, vec_stored = sem("vec_made"), sem("vec_copied"), sem("vec_stored")
        in_hi, in_lo = sem("in_hi"), sem("in_lo")
        eps_set, table_set = sem("eps_set"), sem("table_set")
        a_first_done, b_first_done = sem("a_first_done"), sem("b_first_done")
        gained = sem("gained")
        upper_copied, summed = sem("upper_copied"), sem("summed")
        b_gated, z_gated, gate_ready = sem("b_gated"), sem("z_gated"), sem("gate_ready")
        u_ready, taps_copied, tap_done = sem("u_ready"), sem("taps_copied"), sem("tap_done")
        mean_ready, centered, squared, var_part = sem("mean_ready"), sem("centered"), sem("squared"), sem("var_part")
        ln_std_ready, ln_rstd_ready = sem("ln_std_ready"), sem("ln_rstd_ready")
        ln_scaled, swished, y_ready, y_hi, y_lo = (
            sem("ln_scaled"), sem("swished"), sem("y_ready"), sem("y_hi"), sem("y_lo"))
        x1_added, x1_squared, x1_summed, resid_stored = (
            sem("x1_added"), sem("x1_squared"), sem("x1_summed"), sem("resid_stored"))
        x1_std, x1_rstd, x1_normed, x1_turned = sem("x1_std"), sem("x1_rstd"), sem("x1_normed"), sem("x1_turned")
        kv_hi, kv_lo, qb_hi, qb_lo = sem("kv_hi"), sem("kv_lo"), sem("qb_hi"), sem("qb_lo")
        bias_loaded, bias_added, max_ready, exp_done = (
            sem("bias_loaded"), sem("bias_added"), sem("max_ready"), sem("exp_done"))
        scores_done, v_turned, v_copied = sem("scores_done"), sem("v_turned"), sem("v_copied")
        z_tanh_ready, z_gate_ready = sem("z_tanh_ready"), sem("z_gate_ready")
        row_maxed, rden_ready, prob_ready, prob_turned, prob_copied = (
            sem("row_maxed"), sem("rden_ready"), sem("prob_ready"), sem("prob_turned"), sem("prob_copied"))
        attended, y2_ready, y2_hi, y2_lo = sem("attended"), sem("y2_ready"), sem("y2_hi"), sem("y2_lo")
        resid_in, gain_in = sem("resid_in"), sem("gain_in")
        x2_added, x2_squared, x2_summed, x2_std, x2_rstd = (
            sem("x2_added"), sem("x2_squared"), sem("x2_summed"), sem("x2_std"), sem("x2_rstd"))
        out_ready, out_stored = sem("out_ready"), sem("out_stored")
        act_out_ready = sem("act_out_ready")

        sq_sum = stat[:, 0:2]
        std = stat[:, 2:4]
        rstd = stat[:, 4:6]
        sq_part = stat[:, 6:14].rearrange("p (t c) -> p t c", t=TT)
        row_max = stat[:, 14:16]
        neg_max = stat[:, 16:18]
        den = stat[:, 18:20]
        rden = stat[:, 20:22]
        scrap = stat[:, 22:23]
        eps = stat[:, 23:24]

        def load_slab(sp, stream, turn, j, src):
            slot = stream.slot(j)
            if isinstance(turn, int) and turn == 0 and j < stream.ring:
                before = {id(CONV): None, id(A_OUT): CONV, id(QKV): A_OUT, id(B_OUT): QKV}[id(stream)]
                if before is not None:
                    last = 2 * (before.count + j - stream.ring + 1)
                    sp.wait_ge(lo_dve if before is QKV else lo_pool, before.lo_base + last)
            else:
                sp.wait_ge(lo_dve if stream is QKV else lo_pool,
                           stream.lo_halves(turn, 2 * (j - stream.ring) + 1))
            sp.dma_start(raw[:, slot, :], src).then_inc(raw_in[slot], 16)

        def split_hi(act, stream, turn, j, halves=(0, 1)):
            slot = stream.slot(j)
            loads = fills(stream, slot) + j // stream.ring + 1
            for half in (2 * j + n for n in halves):
                part = (half % 2) * HALF
                if half % 2 == 0:
                    act.wait_ge(raw_in[slot], 16 * (turn * (stream.per_turn // stream.ring) + loads))
                positive(act, mm_done, stream.mm_halves(turn, half - stream.half_ring))
                nc.scalar.activation(w_hi[:, stream.half_slot(half), :], raw[:, slot, part:part + HALF],
                                     ACT.Copy).then_inc(hi_done, 1)

        def split_lo(eng, stream, turn, j, done, halves=(0, 1)):
            slot = stream.slot(j)
            for half in (2 * j + n for n in halves):
                part = (half % 2) * HALF
                eng.wait_ge(hi_done, stream.mm_halves(turn, half))
                eng.tensor_tensor(w_lo[:, stream.half_slot(half), :], raw[:, slot, part:part + HALF],
                                  w_hi[:, stream.half_slot(half), :].bitcast(F32),
                                  ALU.subtract).then_inc(done, 1)

        def project(pe, stream, turn, j, dst, source, source_ready=None):
            for half in (2 * j, 2 * j + 1):
                slot = stream.half_slot(half)
                pe.wait_ge(lo_dve if stream is QKV else lo_pool, stream.lo_halves(turn, half))
                for k in range(KT // 2):
                    kt = (half % 2) * (KT // 2) + k
                    if source_ready is not None:
                        pe.wait_ge(source_ready, kt + 1)
                    nc.tensor.matmul(dst[:, 0:2 * S], w_hi[:, slot, k * P:(k + 1) * P],
                                     source[:, kt, :, :], start=(kt == 0), stop=False)
                    mm = nc.tensor.matmul(dst[:, 0:S], w_lo[:, slot, k * P:(k + 1) * P],
                                          source[:, kt, 0, :], start=False, stop=(kt == KT - 1))
                mm.then_inc(mm_done, 1)

        def out_project(pe, stream, c, q, banks, source, ready):
            for half in (2 * q, 2 * q + 1):
                slot = stream.half_slot(half)
                pe.wait_ge(lo_pool, stream.lo_halves(c, half))
                for k in range(RKT // 2):
                    kt = half * (RKT // 2) + k
                    if ready is not None:
                        pe.wait_ge(ready, kt + 1)
                    wide_hi = w_hi[:, slot, k * CHUNK:(k + 1) * CHUNK]
                    wide_lo = w_lo[:, slot, k * CHUNK:(k + 1) * CHUNK]
                    for t in range(TT):
                        y_h, y_l = (source[:, kt, part, t * P:(t + 1) * P] for part in (0, 1))
                        nc.tensor.matmul(banks[t][:, :], y_h, wide_hi, start=(kt == 0), stop=False)
                        nc.tensor.matmul(banks[t][:, :], y_h, wide_lo, start=False, stop=False)
                        mm = nc.tensor.matmul(banks[t][:, :], y_l, wide_hi, start=False, stop=(kt == KT - 1))
                mm.then_inc(mm_done, 1)

        def out_project_last(pe, stream, banks, source, first_done):
            c, q = CHUNKS - 1, stream.per_turn - 1
            for t in range(TT):
                for half in (2 * q, 2 * q + 1):
                    slot = stream.half_slot(half)
                    if t == 0:
                        pe.wait_ge(lo_pool, stream.lo_halves(c, half))
                    for k in range(RKT // 2):
                        kt = half * (RKT // 2) + k
                        wide_hi = w_hi[:, slot, k * CHUNK:(k + 1) * CHUNK]
                        wide_lo = w_lo[:, slot, k * CHUNK:(k + 1) * CHUNK]
                        y_h, y_l = (source[:, kt, part, t * P:(t + 1) * P] for part in (0, 1))
                        nc.tensor.matmul(banks[t][:, :], y_h, wide_hi, start=False, stop=False)
                        nc.tensor.matmul(banks[t][:, :], y_h, wide_lo, start=False, stop=False)
                        mm = nc.tensor.matmul(banks[t][:, :], y_l, wide_hi, start=False, stop=(kt == KT - 1))
                    if t == TT - 1:
                        mm.then_inc(mm_done, 1)
                if t == 0:
                    mm.then_inc(first_done, 1)

        w_in_cols = a_w_in[0].rearrange("(kt p) n -> p kt n", p=P)
        kv_cols = w_kv.rearrange("(kt p) n -> p kt n", p=P)
        q_cols = b_w_in[0].rearrange("(kt p) n -> p kt n", p=P)

        def out_slab(w, c, q):
            return w.rearrange("(kt p) n -> p kt n", p=P)[:, q * RKT:(q + 1) * RKT, c * CHUNK:(c + 1) * CHUNK]

        def head_slab(j, first_col):
            if j < 2 * NG:
                v, g = divmod(j, NG)
                return kv_cols[:, :, bass.ds(first_col + (2 * g + v) * D, P)]
            return q_cols[:, :, bass.ds(first_col + (j - 2 * NG) * D, P)]

        param_sources = ((0, a_conv_w[0]), (ROW_CONV_B, a_conv_b), (ROW_LN_G, a_ln_g), (ROW_LN_B, a_ln_b),
                         (ROW_A_NORM, a_norm), (ROW_KV_NORM, kv_norm.rearrange("(a n) -> a n", a=1)),
                         (ROW_B_NORM, b_norm))

        block = ctx.enter_context(nc.Block())

        @block.sync
        def _(sp):
            x_rows = x.rearrange("b (t p) d -> p (b t) d", p=P)
            for t in range(TT):
                sp.dma_start(x_sb[:, t, :], x_rows[:, t, :]).then_inc(x_in[t], 16)
            for first, src in param_sources[:4]:
                sp.dma_start(param_rows[first:first + src.shape[0], :], src).then_inc(rows_in, 16)
            for j in range(3):
                load_slab(sp, CONV, 0, j, w_in_cols[:, :, j * D:j * D + P])
            sp.dma_start(buckets, bucket_rows).then_inc(bias_in, 16)
            sp.dma_start(rel[0:BUCKETS, :], rel_bias).then_inc(bias_in, 16)
            with sp.Fori(1, KT) as c:
                cols = [sp.snap(c * P + j * D) for j in range(3)]
                for j in range(3):
                    load_slab(sp, CONV, c, j, w_in_cols[:, :, bass.ds(cols[j], P)])
            sp.wait_ge(vec_copied, NG)
            sp.dma_start(bias_dram.ap(), bias_vec).then_inc(vec_stored, 16)
            sp.wait_ge(vec_stored, 16)
            for c in range(CHUNKS):
                for q in range(A_OUT.per_turn):
                    load_slab(sp, A_OUT, c, q, out_slab(a_w_out[0], c, q))

            def load_bias(first):
                src = bass.AP(bias_dram, first, [[1, P], [BIAS_W, NG], [1, S]])
                sp.dma_start(bias[:, :, :], src).then_inc(bias_loaded, 16)

            for j in range(QKV.per_turn):
                load_slab(sp, QKV, 0, j, head_slab(j, 0))
                if j == 1:
                    sp.wait_ge(x1_turned, TT * KT)
                    sp.dma_start(resid_dram.ap(), x_sb[:, :, :]).then_inc(resid_stored, 16)
            load_bias(P)
            with sp.Fori(1, HEADS) as h:
                col = sp.snap(h * P)
                cols = [sp.snap(col + (2 * (j % NG) + j // NG) * D) if j < 2 * NG
                        else sp.snap(col + (j - 2 * NG) * D) for j in range(QKV.per_turn)]
                first = sp.snap(h * (NG * BIAS_W) + P)
                for j in range(QKV.per_turn):
                    w = kv_cols if j < 2 * NG else q_cols
                    load_slab(sp, QKV, h, j, w[:, :, bass.ds(cols[j], P)])
                sp.wait_ge(bias_added, 3 * h)
                load_bias(first)
            for c in range(CHUNKS):
                for q in range(B_OUT.per_turn):
                    load_slab(sp, B_OUT, c, q, out_slab(b_w_out[0], c, q))
                    if (c, q) == (0, 1):
                        sp.wait_ge(mm_done, QKV.mm_halves(HEADS - 1, 2 * QKV.per_turn - 1))
                        sp.wait_ge(resid_stored, 16)
                        sp.dma_start(resid[:, :, :], resid_dram.ap()).then_inc(resid_in, 16)
                        sp.dma_start(gain_row[:, :], final_norm.rearrange("(a n) -> a n", a=1)
                                     .partition_broadcast(P)[:, 0, :]).then_inc(gain_in, 16)
            out_rows = out.rearrange("b (t p) d -> p (b t) d", p=P)
            for t in range(TT):
                for half in range(2):
                    cols = slice(half * (D // 2), (half + 1) * (D // 2))
                    if (t, half) == (1, 1):
                        sp.wait_ge(act_out_ready, 1)
                    else:
                        sp.wait_ge(out_ready, 2 * t + half + 1)
                    sp.dma_start(out_rows[:, t, cols], rows[:, t, cols]).then_inc(out_stored, 16)
            sp.wait_ge(out_stored, 16 * 2 * TT)

        @block.gpsimd
        def _(pool):
            nc.gpsimd.memset(raw[BUCKETS:BUCKETS + 1, 0, NG * BIAS_W:NG * BIAS_W + HEADS],
                             MASKED).then_inc(rel_mask, 1)
            pool.wait_ge(rel_mask, 1)
            nc.gpsimd.memset(ident[:, :], 0.0).then_inc(consts, 1)
            nc.gpsimd.memset(mean_w[:, :], 1.0 / D).then_inc(consts, 1)
            pool.wait_ge(consts, 2)
            nc.gpsimd.affine_select(out=ident[:, :], in_=ident[:, :], compare_op=ALU.not_equal, fill=1.0,
                                    base=0, pattern=[[-1, P]], channel_multiplier=1).then_inc(consts, 1)
            with pool.Fori(0, KT) as c:
                for j in range(3):
                    split_lo(pool, CONV, c, j, lo_pool)
            with pool.Fori(0, CHUNKS) as c:
                for q in range(A_OUT.per_turn):
                    split_lo(pool, A_OUT, c, q, lo_pool)
            with pool.Fori(0, CHUNKS) as c:
                for q in range(B_OUT.per_turn):
                    split_lo(pool, B_OUT, c, q, lo_pool)

        @block.scalar
        def _(act):
            for first, src in param_sources[4:]:
                act.dma_start(param_rows[first:first + src.shape[0], :], src).then_inc(rows_in, 16)

            act.wait_ge(eps_set, 2)
            nc.scalar.activation(scrap, eps, ACT.Sqrt).then_inc(table_set, 1)
            for t in range(TT):
                act.wait_ge(x_in[t], 16)
                nc.scalar.activation(xn[:, t, :], x_sb[:, t, :], ACT.Square,
                                     accum_out=sq_sum[:, t:t + 1]).then_inc(x_squared, 1)
                act.wait_ge(x_squared, t + 1)
                nc.scalar.activation(std[:, t:t + 1], sq_sum[:, t:t + 1], ACT.Sqrt, bias=eps,
                                     scale=1.0 / D).then_inc(std_ready, 1)
            act.wait_ge(table_set, 1)
            nc.scalar.activation(scrap, eps, ACT.Sigmoid).then_inc(table_set, 1)
            split_hi(act, CONV, 0, 0)
            act.wait_ge(param_ready, 2)
            for kt in range(KT):
                act.wait_ge(x_turned, KT + 2 * (kt // 2 + 1))
                nc.scalar.activation(act_a[:, kt, 0, :], bank[kt // 2][:, (kt % 2) * S:(kt % 2 + 1) * S],
                                     ACT.Copy, scale=param[:, kt, ROW_A_NORM:ROW_A_NORM + 1]).then_inc(in_hi, 1)
                if kt in (9, 13):
                    split_hi(act, CONV, 0, 1, halves=((kt - 9) // 4,))

            def copy_upper(c, j):
                act.wait_ge(mm_done, CONV.mm_halves(c, 2 * j + 1))
                if j == 0:
                    positive(act, summed, 3 * c - 2)
                else:
                    act.wait_ge(summed, 3 * c + 1)
                nc.scalar.activation(upper[:, j, :], bank[j][:, S:2 * S], ACT.Copy).then_inc(upper_copied, 1)

            def gate_b(c):
                act.wait_ge(summed, 3 * c + 2)
                nc.scalar.activation(b_sig[:, :], b_sum[:, :], ACT.Sigmoid).then_inc(b_gated, 1)

            def gate_z(c):
                act.wait_ge(summed, 3 * c + 3)
                nc.scalar.activation(z_sig[:, :], z_sum[:, :], ACT.Sigmoid).then_inc(z_gated, 1)

            split_hi(act, CONV, 0, 2)
            copy_upper(0, 0)
            with act.Fori(1, KT) as c:
                split_hi(act, CONV, c, 0)
                copy_upper(c - 1, 1)
                split_hi(act, CONV, c, 1)
                gate_b(c - 1)
                copy_upper(c - 1, 2)
                split_hi(act, CONV, c, 2)
                gate_z(c - 1)
                copy_upper(c, 0)
            split_hi(act, A_OUT, 0, 0)
            copy_upper(KT - 1, 1)
            gate_b(KT - 1)
            split_hi(act, A_OUT, 0, 1)
            copy_upper(KT - 1, 2)
            gate_z(KT - 1)

            for q in range(4):
                act.wait_ge(centered, q + 1)
                nc.scalar.activation(squares[:, q, :, :], conv[:, 4 * q:4 * q + 4, :],
                                     ACT.Square).then_inc(squared, 1)
            act.wait_ge(var_part, 4)
            nc.scalar.activation(ln_std[:, :], bank[5][:, 0:S], ACT.Sqrt,
                                 bias=eps).then_inc(ln_std_ready, 1)
            for kt in range(KT + 1):
                if kt < KT:
                    act.wait_ge(ln_scaled, kt + 1)
                    nc.scalar.activation(conv[:, kt, :], conv[:, kt, :], ACT.Silu,
                                         bias=param[:, kt, ROW_LN_B:ROW_LN_B + 1],
                                         scale=param[:, kt, ROW_LN_G:ROW_LN_G + 1]).then_inc(swished, 1)
                if kt > 0:
                    act.wait_ge(y_ready, kt)
                    nc.scalar.activation(act_a[:, kt - 1, 0, :], conv[:, kt - 1, :], ACT.Copy).then_inc(y_hi, 1)
                if kt in Y_LOOP_SPLITS:
                    split_hi(act, A_OUT, 0, *Y_LOOP_SPLITS[kt])

            def square_rows(c, t):
                cols = slice(c * CHUNK, (c + 1) * CHUNK)
                act.wait_ge(x1_added, TT * c + t + 1)
                nc.scalar.activation(xn[:, t, cols], x_sb[:, t, cols], ACT.Square,
                                     accum_out=sq_part[:, t, c:c + 1]).then_inc(x1_squared, 1)

            for n in range(3, A_OUT.count):
                c, q = divmod(n, A_OUT.per_turn)
                split_hi(act, A_OUT, c, q)
                if n == 3:
                    act.wait_ge(table_set, 2)
                    nc.scalar.activation(scrap, eps, ACT.Sqrt).then_inc(table_set, 1)
                if q == 2 and c > 0:
                    for t in range(TT):
                        square_rows(c - 1, t)
            split_hi(act, QKV, 0, 0)
            for t in range(TT):
                square_rows(CHUNKS - 1, t)
                act.wait_ge(x1_summed, t + 1)
                nc.scalar.activation(std[:, t:t + 1], sq_sum[:, t:t + 1], ACT.Sqrt, bias=eps,
                                     scale=1.0 / D).then_inc(x1_std, 1)
            split_hi(act, QKV, 0, 1, halves=(0,))

            def kv_input(kt):
                act.wait_ge(x1_turned, KT + 2 * (kt // 2 + 1))
                nc.scalar.activation(act_a[:, kt, 0, ::-1], bank[kt // 2][:, (kt % 2) * S:(kt % 2 + 1) * S],
                                     ACT.Copy, scale=param[:, kt, ROW_KV_NORM:ROW_KV_NORM + 1]).then_inc(kv_hi, 1)

            def q_input(kt):
                act.wait_ge(kv_lo, 2 * (kt // 2 + 1))
                nc.scalar.activation(act_b[:, kt, 0, :], bank[kt // 2][:, (kt % 2) * S:(kt % 2 + 1) * S],
                                     ACT.Copy, scale=param[:, kt, ROW_B_NORM:ROW_B_NORM + 1]).then_inc(qb_hi, 1)

            for step, tiles in INPUT_ORDER:
                for kt in tiles:
                    (kv_input if step == "kv" else q_input)(kt)
            split_hi(act, QKV, 0, 1, halves=(1,))

            def copy_upper_head(h, j):
                act.wait_ge(mm_done, QKV.mm_halves(h, 2 * j + 1))
                positive(act, summed, 3 * KT + h * QKV.per_turn + (j - 1))
                nc.scalar.activation(upper[:, j % 2, :], bank[j % 2][:, S:2 * S], ACT.Copy).then_inc(upper_copied, 1)

            def tanh_gate(h):
                act.wait_ge(summed, 3 * KT + (h + 1) * QKV.per_turn)
                nc.scalar.activation(z_tanh[:, :], z_t[:, :], ACT.Tanh, scale=0.5).then_inc(z_tanh_ready, 1)

            def copy_v(h):
                act.wait_ge(v_turned, h + 1)
                for b, (g0, n) in enumerate(((0, 2), (2, 1))):
                    nc.scalar.activation(v_rows[:, g0:g0 + n, :, :].rearrange("p g t d -> p (g t d)"),
                                         bank[5 + b][:, 0:n * S], ACT.Copy).then_inc(v_copied, 1)

            def exps(h):
                act.wait_ge(max_ready, h + 1)
                nc.scalar.activation(prob[:, 0:NG * P], prob[:, 0:NG * P], ACT.Exp, bias=neg_max[:, 0:1],
                                     accum_out=den[:, 0:1]).then_inc(exp_done, 1)
                nc.scalar.activation(prob[:, NG * P:], prob[:, NG * P:], ACT.Exp, bias=neg_max[:, 1:2],
                                     accum_out=den[:, 1:2]).then_inc(exp_done, 1)

            def copy_probs(h):
                act.wait_ge(prob_turned, h + 1)
                for g in range(NG):
                    nc.scalar.activation(prob_t[:, g, :], bank[2 + g][:, 0:3 * P], ACT.Copy).then_inc(prob_copied, 1)

            for j in range(2, QKV.per_turn):
                split_hi(act, QKV, 0, j)
                for kt in LATE_Q_INPUT.get(j, ()):
                    q_input(kt)
                copy_upper_head(0, j - 2)
                if j == 5:
                    act.wait_ge(table_set, 3)
                    nc.scalar.activation(scrap, eps, ACT.Exp).then_inc(table_set, 1)
            with act.Fori(1, HEADS) as h:
                for j in range(QKV.per_turn):
                    split_hi(act, QKV, h, j)
                    if j < 2:
                        copy_upper_head(h - 1, j + QKV.per_turn - 2)
                    else:
                        copy_upper_head(h, j - 2)
                    if j == 2:
                        copy_v(h - 1)
                        tanh_gate(h - 1)
                    if j == 3:
                        exps(h - 1)
                    if j == 6:
                        copy_probs(h - 1)
            last = HEADS - 1
            split_hi(act, B_OUT, 0, 0)
            copy_upper_head(last, QKV.per_turn - 2)
            split_hi(act, B_OUT, 0, 1)
            copy_upper_head(last, QKV.per_turn - 1)
            act.wait_ge(y2_ready, last)
            for kt in range(last):
                nc.scalar.activation(act_a[:, kt, 0, :], y2[:, kt, :], ACT.Copy).then_inc(y2_hi, 1)
            copy_v(last)
            tanh_gate(last)
            exps(last)
            split_hi(act, B_OUT, 0, 2)
            copy_probs(last)
            split_hi(act, B_OUT, 0, 3)
            act.wait_ge(y2_ready, HEADS)
            nc.scalar.activation(act_a[:, last, 0, :], y2[:, last, :], ACT.Copy).then_inc(y2_hi, 1)

            def square_out(c, t):
                act.wait_ge(x2_added, TT * c + t + 1)
                if c > 0:
                    act.wait_ge(x2_squared, TT * (c - 1) + t + 1)
                nc.scalar.activation(bank[4 + t][:, :], resid[:, t, c * CHUNK:(c + 1) * CHUNK], ACT.Square,
                                     accum_out=sq_part[:, t, c:c + 1]).then_inc(x2_squared, 1)

            for n in range(B_OUT.per_turn, B_OUT.count):
                c, q = divmod(n, B_OUT.per_turn)
                split_hi(act, B_OUT, c, q)
                if n == B_OUT.per_turn:
                    act.wait_ge(table_set, 4)
                    nc.scalar.activation(scrap, eps, ACT.Sqrt).then_inc(table_set, 1)
                if q == 2 and c > 0:
                    for t in range(TT):
                        square_out(c - 1, t)
            for t in range(TT):
                square_out(CHUNKS - 1, t)
                act.wait_ge(x2_summed, t + 1)
                nc.scalar.activation(std[:, t:t + 1], sq_sum[:, t:t + 1], ACT.Sqrt, bias=eps,
                                     scale=1.0 / D).then_inc(x2_std, 1)
            act.wait_ge(x2_rstd, TT)
            act.wait_ge(gained, TT * CHUNKS)
            nc.scalar.activation(rows[:, 1, D // 2:], rows[:, 1, D // 2:], ACT.Copy,
                                 scale=rstd[:, 1:2]).then_inc(act_out_ready, 1)

        @block.vector
        def _(dve):
            nc.vector.memset(eps, EPS).then_inc(eps_set, 1)
            nc.vector.memset(u[:, 0:TAPS - 1], 0.0).then_inc(eps_set, 1)
            def scale_rows(t, std_sem, rstd_sem, normed_sem):
                dve.wait_ge(std_sem, t + 1)
                nc.vector.reciprocal(rstd[:, t:t + 1], std[:, t:t + 1]).then_inc(rstd_sem, 1)
                dve.wait_ge(rstd_sem, t + 1)
                for cols in (slice(0, D // 2), slice(D // 2, D)):
                    nc.vector.tensor_scalar(xn[:, t, cols], x_sb[:, t, cols], rstd[:, t:t + 1], None,
                                            ALU.mult).then_inc(normed_sem, 1)

            scale_rows(0, std_ready, rstd_ready, x_normed)
            for b in range(2):
                dve.wait_ge(rows_turned, b + 1)
                nc.vector.tensor_copy(param[:, 8 * b:8 * b + 8, :].rearrange("p k r -> p (k r)"),
                                      bank[6 + b][:, 0:8 * ROWS]).then_inc(param_ready, 1)
            scale_rows(1, std_ready, rstd_ready, x_normed)
            for kt in range(KT):
                dve.wait_ge(in_hi, 2 * (kt // 2 + 1))
                if kt == 0:
                    dve.wait_ge(param_ready, 2)
                nc.vector.scalar_tensor_tensor(
                    out=act_a[:, kt, 1, :], in0=bank[kt // 2][:, (kt % 2) * S:(kt % 2 + 1) * S],
                    scalar=param[:, kt, ROW_A_NORM:ROW_A_NORM + 1], in1=act_a[:, kt, 0, :].bitcast(F32),
                    op0=ALU.mult, op1=ALU.subtract).then_inc(in_lo, 1)
            def add_halves(c, j, dst):
                dve.wait_ge(upper_copied, 3 * c + (j + 1))
                nc.vector.tensor_tensor(dst, bank[j][:, 0:S], upper[:, j, :], ALU.add).then_inc(summed, 1)

            def tap(c, k):
                acc = bank[3][:, (k % 2) * S:(k % 2 + 1) * S]
                if k >= 2:
                    dve.wait_ge(tap_done, c * (TAPS + 1) + (k - 1))
                if k == 0:
                    nc.vector.tensor_scalar(acc, u[:, k:k + S], taps[:, k:k + 1], taps[:, TAPS:TAPS + 1],
                                            ALU.mult, ALU.add).then_inc(tap_done, 1)
                elif k == 1:
                    nc.vector.tensor_scalar(acc, u[:, k:k + S], taps[:, k:k + 1], None,
                                            ALU.mult).then_inc(tap_done, 1)
                else:
                    nc.vector.scalar_tensor_tensor(out=odd_taps[:, :] if k == TAPS - 2 else acc,
                                                   in0=u[:, k:k + S], scalar=taps[:, k:k + 1], in1=acc,
                                                   op0=ALU.mult, op1=ALU.add).then_inc(tap_done, 1)

            def join_taps(c, dst):
                dve.wait_ge(tap_done, c * (TAPS + 1) + TAPS)
                nc.vector.tensor_tensor(dst, bank[3][:, 0:S], odd_taps[:, :], ALU.add).then_inc(tap_done, 1)

            def load_taps(c, src):
                dve.wait_ge(u_ready, c + 1)
                nc.vector.tensor_copy(taps[:, :], src).then_inc(taps_copied, 1)
                dve.wait_ge(taps_copied, c + 1)

            def glu(c):
                dve.wait_ge(b_gated, c + 1)
                positive(dve, tap_done, c * (TAPS + 1))
                nc.vector.tensor_tensor(u[:, TAPS - 1:], a_sum[:, :], b_sig[:, :], ALU.mult).then_inc(u_ready, 1)

            def gate_out(c, dst):
                dve.wait_ge(z_gated, c + 1)
                nc.vector.tensor_tensor(dst, z_sum[:, :], z_sig[:, :], ALU.mult).then_inc(gate_ready, 1)

            add_halves(0, 0, a_sum[:, :])
            add_halves(0, 1, b_sum[:, :])
            glu(0)
            add_halves(0, 2, z_sum[:, :])
            for g in range(NG):
                dve.wait_ge(vec_made, g + 1)
                nc.vector.tensor_copy(bias_vec[:, g * BIAS_W:(g + 1) * BIAS_W], bank[5 + g][0:HEADS, :]
                                      ).then_inc(vec_copied, 1)
            with dve.Fori(1, KT) as c:
                tile_before = dve.snap(c - 1)
                dve.wait_ge(u_ready, c)
                add_halves(c, 0, a_sum[:, :])
                gate_out(c - 1, gate[:, bass.ds(tile_before, 1), :].rearrange("p a s -> p (a s)"))
                load_taps(c - 1, param[:, bass.ds(tile_before, 1), 0:TAPS + 1].rearrange("p a r -> p (a r)"))
                for k in range(16):
                    tap(c - 1, k)
                dve.wait_ge(b_gated, c)
                add_halves(c, 1, b_sum[:, :])
                for k in range(16, TAPS):
                    tap(c - 1, k)
                join_taps(c - 1, conv[:, bass.ds(tile_before, 1), :].rearrange("p a s -> p (a s)"))
                glu(c)
                dve.wait_ge(gate_ready, c)
                add_halves(c, 2, z_sum[:, :])
            last = KT - 1
            load_taps(last, param[:, last, 0:TAPS + 1])
            for k in range(TAPS):
                tap(last, k)
            join_taps(last, conv[:, last, :])
            gate_out(last, gate[:, last, :])

            dve.wait_ge(mean_ready, 1)
            for q in range(4):
                mean = bank[4][:, 0:S].unsqueeze(1).to_broadcast([P, 4, S])
                nc.vector.tensor_tensor(conv[:, 4 * q:4 * q + 4, :], conv[:, 4 * q:4 * q + 4, :], mean,
                                        ALU.subtract).then_inc(centered, 1)
            dve.wait_ge(ln_std_ready, 1)
            nc.vector.reciprocal(ln_rstd[:, :], ln_std[:, :]).then_inc(ln_rstd_ready, 1)
            dve.wait_ge(ln_rstd_ready, 1)
            dve.wait_ge(squared, 4)
            dve.wait_ge(gate_ready, KT)
            for kt in range(KT + 2):
                if kt < KT:
                    nc.vector.tensor_tensor(conv[:, kt, :], conv[:, kt, :], ln_rstd[:, :],
                                            ALU.mult).then_inc(ln_scaled, 1)
                if 1 <= kt <= KT:
                    dve.wait_ge(swished, kt)
                    nc.vector.tensor_tensor(conv[:, kt - 1, :], conv[:, kt - 1, :], gate[:, kt - 1, :],
                                            ALU.mult).then_inc(y_ready, 1)
                if kt >= 2:
                    dve.wait_ge(y_hi, kt - 1)
                    nc.vector.tensor_tensor(act_a[:, kt - 2, 1, :], conv[:, kt - 2, :],
                                            act_a[:, kt - 2, 0, :].bitcast(F32), ALU.subtract).then_inc(y_lo, 1)

            def wait_chunk(stream, c, t, first_done):
                if c == CHUNKS - 1 and t == 0:
                    dve.wait_ge(first_done, 1)
                else:
                    dve.wait_ge(mm_done, stream.mm_halves(c, 2 * stream.per_turn - 1))

            def sum_squares(t, squared_sem, summed_sem):
                dve.wait_ge(squared_sem, TT * (CHUNKS - 1) + t + 1)
                nc.vector.tensor_reduce(sq_sum[:, t:t + 1], sq_part[:, t, :], AX.X, ALU.add).then_inc(summed_sem, 1)

            def add_layer0(c, t):
                wait_chunk(A_OUT, c, t, a_first_done)
                cols = x_sb[:, t, c * CHUNK:(c + 1) * CHUNK]
                nc.vector.tensor_tensor(cols, bank[2 * (c % 2) + t][:, :], cols, ALU.add).then_inc(x1_added, 1)

            for c in range(CHUNKS - 1):
                for t in range(TT):
                    add_layer0(c, t)
            split_lo(dve, QKV, 0, 0, lo_dve)
            add_layer0(CHUNKS - 1, 0)
            sum_squares(0, x1_squared, x1_summed)
            dve.wait_ge(x1_added, TT * (CHUNKS - 1) + 1)
            scale_rows(0, x1_std, x1_rstd, x1_normed)
            add_layer0(CHUNKS - 1, 1)
            sum_squares(1, x1_squared, x1_summed)
            dve.wait_ge(x1_added, TT * CHUNKS)
            scale_rows(1, x1_std, x1_rstd, x1_normed)
            split_lo(dve, QKV, 0, 1, lo_dve, halves=(0,))

            def kv_input(kt):
                dve.wait_ge(kv_hi, 2 * (kt // 2 + 1))
                nc.vector.scalar_tensor_tensor(
                    out=act_a[:, kt, 1, ::-1], in0=bank[kt // 2][:, (kt % 2) * S:(kt % 2 + 1) * S],
                    scalar=param[:, kt, ROW_KV_NORM:ROW_KV_NORM + 1], in1=act_a[:, kt, 0, ::-1].bitcast(F32),
                    op0=ALU.mult, op1=ALU.subtract).then_inc(kv_lo, 1)

            def q_input(kt):
                dve.wait_ge(qb_hi, 2 * (kt // 2 + 1))
                nc.vector.scalar_tensor_tensor(
                    out=act_b[:, kt, 1, :], in0=bank[kt // 2][:, (kt % 2) * S:(kt % 2 + 1) * S],
                    scalar=param[:, kt, ROW_B_NORM:ROW_B_NORM + 1], in1=act_b[:, kt, 0, :].bitcast(F32),
                    op0=ALU.mult, op1=ALU.subtract).then_inc(qb_lo, 1)

            for step, tiles in INPUT_ORDER:
                for kt in tiles:
                    (kv_input if step == "kv" else q_input)(kt)
            split_lo(dve, QKV, 0, 1, lo_dve, halves=(1,))

            def head_sum(h, j):
                dst = [k_t, v_t, q_t][j // NG][:, j % NG, :] if j < 3 * NG else z_t[:, :]
                dve.wait_ge(upper_copied, 3 * KT + h * QKV.per_turn + (j + 1))
                nc.vector.tensor_tensor(dst, bank[j % 2][:, 0:S], upper[:, j % 2, :], ALU.add).then_inc(summed, 1)

            def biased_scores(h):
                dve.wait_ge(scores_done, h + 1)
                dve.wait_ge(bias_loaded, 16 * (h + 1))
                nc.vector.scalar_tensor_tensor(
                    out=prob[:, 0:NG * P].rearrange("p (g k) -> p g k", g=NG),
                    in0=bank[2][:, 0:NG * P].rearrange("p (g k) -> p g k", g=NG), scalar=SCALE,
                    in1=bias[:, :, 0:P], op0=ALU.mult, op1=ALU.add).then_inc(bias_added, 1)
                nc.vector.scalar_tensor_tensor(
                    out=prob[:, NG * P:NG * P + 2 * S].rearrange("p (g k) -> p g k", g=2),
                    in0=bank[3][:, 0:2 * S].rearrange("p (g k) -> p g k", g=2), scalar=SCALE,
                    in1=bias[:, 0:2, :], op0=ALU.mult, op1=ALU.add).then_inc(bias_added, 1)
                nc.vector.scalar_tensor_tensor(
                    out=prob[:, NG * P + 2 * S:], in0=bank[4][:, 0:S], scalar=SCALE,
                    in1=bias[:, 2, :], op0=ALU.mult, op1=ALU.add).then_inc(bias_added, 1)
                for t, cols in enumerate((prob[:, 0:NG * P], prob[:, NG * P:])):
                    dve.wait_ge(bias_added, 3 * h + (1 if t == 0 else 3))
                    nc.vector.tensor_reduce(row_max[:, t:t + 1], cols, AX.X, ALU.max).then_inc(row_maxed, 1)
                dve.wait_ge(row_maxed, 2 * (h + 1))
                nc.vector.tensor_scalar(neg_max, row_max, -1.0, None, ALU.mult).then_inc(max_ready, 1)

            def normalise(h):
                dve.wait_ge(exp_done, 2 * (h + 1))
                nc.vector.reciprocal(rden, den).then_inc(rden_ready, 1)
                dve.wait_ge(rden_ready, h + 1)
                for t, cols in enumerate((prob[:, 0:NG * P], prob[:, NG * P:])):
                    nc.vector.tensor_scalar(cols, cols, rden[:, t:t + 1], None, ALU.mult).then_inc(prob_ready, 1)

            def gated(h, dst):
                dve.wait_ge(z_tanh_ready, h + 1)
                nc.vector.scalar_tensor_tensor(out=z_gate[:, :], in0=z_tanh[:, :], scalar=1.0, in1=z_t[:, :],
                                               op0=ALU.add, op1=ALU.mult).then_inc(z_gate_ready, 1)
                dve.wait_ge(z_gate_ready, h + 1)
                dve.wait_ge(attended, h + 1)
                nc.vector.scalar_tensor_tensor(out=dst, in0=bank[7][:, 0:S], scalar=0.5, in1=z_gate[:, :],
                                               op0=ALU.mult, op1=ALU.mult).then_inc(y2_ready, 1)

            for j in range(2, QKV.per_turn):
                split_lo(dve, QKV, 0, j, lo_dve)
                for kt in LATE_Q_INPUT.get(j, ()):
                    q_input(kt)
                if j == 2:
                    dve.wait_ge(x1_turned, TT * KT)
                head_sum(0, j - 2)
            with dve.Fori(1, HEADS) as h:
                head_before = dve.snap(h - 1)
                for j in range(QKV.per_turn):
                    split_lo(dve, QKV, h, j, lo_dve)
                    if j < 2:
                        head_sum(h - 1, j + QKV.per_turn - 2)
                    else:
                        if j == 2:
                            dve.wait_ge(scores_done, h)
                        if j == 5:
                            dve.wait_ge(v_turned, h)
                        head_sum(h, j - 2)
                    if j == 2:
                        biased_scores(h - 1)
                    if j == 4:
                        normalise(h - 1)
                    if j == 9:
                        gated(h - 1, y2[:, bass.ds(head_before, 1), :].rearrange("p a s -> p (a s)"))
            last = HEADS - 1
            head_sum(last, QKV.per_turn - 2)
            head_sum(last, QKV.per_turn - 1)
            for kt in range(last):
                dve.wait_ge(y2_hi, kt + 1)
                nc.vector.tensor_tensor(act_a[:, kt, 1, :], y2[:, kt, :], act_a[:, kt, 0, :].bitcast(F32),
                                        ALU.subtract).then_inc(y2_lo, 1)
            biased_scores(last)
            normalise(last)
            gated(last, y2[:, last, :])
            dve.wait_ge(y2_hi, HEADS)
            nc.vector.tensor_tensor(act_a[:, last, 1, :], y2[:, last, :], act_a[:, last, 0, :].bitcast(F32),
                                    ALU.subtract).then_inc(y2_lo, 1)

            def add_layer1(c, t):
                wait_chunk(B_OUT, c, t, b_first_done)
                cols = resid[:, t, c * CHUNK:(c + 1) * CHUNK]
                nc.vector.tensor_tensor(cols, bank[2 * (c % 2) + t][:, :], cols, ALU.add).then_inc(x2_added, 1)

            def gain_columns(c, t):
                cols = slice(c * CHUNK, (c + 1) * CHUNK)
                dve.wait_ge(x2_added, TT * c + t + 1)
                nc.vector.tensor_tensor(rows[:, t, cols], resid[:, t, cols], gain_row[:, cols],
                                        ALU.mult).then_inc(gained, 1)

            def rstd_out(t):
                dve.wait_ge(x2_std, t + 1)
                nc.vector.reciprocal(rstd[:, t:t + 1], std[:, t:t + 1]).then_inc(x2_rstd, 1)
                dve.wait_ge(x2_rstd, t + 1)

            def scale_out(t, half):
                cols = slice(half * (D // 2), (half + 1) * (D // 2))
                nc.vector.tensor_scalar(rows[:, t, cols], rows[:, t, cols], rstd[:, t:t + 1], None,
                                        ALU.mult).then_inc(out_ready, 1)

            dve.wait_ge(resid_in, 16)
            dve.wait_ge(gain_in, 16)
            dve.wait_ge(y2_lo, HEADS)
            for c in range(CHUNKS - 1):
                for t in range(TT):
                    add_layer1(c, t)
                for t in range(TT):
                    gain_columns(c, t)
            add_layer1(CHUNKS - 1, 0)
            gain_columns(CHUNKS - 1, 0)
            sum_squares(0, x2_squared, x2_summed)
            rstd_out(0)
            dve.wait_ge(gained, TT * (CHUNKS - 1) + 1)
            scale_out(0, 0)
            scale_out(0, 1)
            add_layer1(CHUNKS - 1, 1)
            gain_columns(CHUNKS - 1, 1)
            sum_squares(1, x2_squared, x2_summed)
            rstd_out(1)
            dve.wait_ge(gained, TT * CHUNKS)
            scale_out(1, 0)

        @block.tensor
        def _(pe):
            pe.wait_ge(consts, 3)

            pe.wait_ge(rows_in, 7 * 16)
            for b in range(2):
                for k in range(8):
                    kt = 8 * b + k
                    mm = nc.tensor.transpose(bank[6 + b][:, k * ROWS:(k + 1) * ROWS],
                                             param_rows[:, kt * P:(kt + 1) * P], ident[0:ROWS, 0:ROWS])
                mm.then_inc(rows_turned, 1)

            def turn_rows(t, normed, turned):
                for kt in range(KT):
                    if kt % (KT // 2) == 0:
                        pe.wait_ge(normed, 2 * t + kt // (KT // 2) + 1)
                    nc.tensor.transpose(bank[kt // 2][:, (kt % 2) * S + t * P:(kt % 2) * S + (t + 1) * P],
                                        xn[:, t, kt * P:(kt + 1) * P], ident[:, :]).then_inc(turned, 1)

            pe.wait_ge(param_ready, 2)
            for t in range(TT):
                turn_rows(t, x_normed, x_turned)

            pe.wait_ge(in_lo, 2)
            for j in range(3):
                if j == 1:
                    pe.wait_ge(in_lo, KT)
                project(pe, CONV, 0, j, bank[j], act_a, in_lo if j == 0 else None)
            pe.wait_ge(bias_in, 32)
            pe.wait_ge(rel_mask, 1)
            for g in range(NG):
                nc.tensor.matmul(bank[5 + g][0:HEADS, :], rel, buckets[:, g * BIAS_W:(g + 1) * BIAS_W],
                                 start=True, stop=True).then_inc(vec_made, 1)
            with pe.Fori(1, KT) as c:
                for j in range(3):
                    pe.wait_ge(summed, 3 * c + (j - 2))
                    project(pe, CONV, c, j, bank[j], act_a)

            for kt in range(KT):
                if kt in (0, KT - 1):
                    pe.wait_ge(tap_done, (TAPS + 1) * (KT - 1 if kt == 0 else KT))
                mm = nc.tensor.matmul(bank[4][:, 0:S], mean_w[:, :], conv[:, kt, :], start=(kt == 0),
                                      stop=(kt == KT - 1))
            mm.then_inc(mean_ready, 1)
            for q in range(4):
                pe.wait_ge(squared, q + 1)
                for k in range(4):
                    mm = nc.tensor.matmul(bank[5][:, 0:S], mean_w[:, :], squares[:, q, k, :],
                                          start=(q + k == 0), stop=(q + k == 6))
                mm.then_inc(var_part, 1)

            for c in range(CHUNKS):
                if c >= 2:
                    pe.wait_ge(x1_added, TT * (c - 1))
                for q in range(A_OUT.per_turn - (c == CHUNKS - 1)):
                    out_project(pe, A_OUT, c, q, bank[2 * (c % 2):2 * (c % 2) + 2], act_a,
                                y_lo if c == 0 else None)
            out_project_last(pe, A_OUT, bank[2:4], act_a, a_first_done)

            pe.wait_ge(x1_added, TT * CHUNKS)
            for t in range(TT):
                turn_rows(t, x1_normed, x1_turned)

            def scores(h):
                pe.wait_ge(summed, 3 * KT + h * QKV.per_turn + (3 * NG))
                for g in range(NG):
                    nc.tensor.matmul(bank[2][:, g * P:(g + 1) * P], q_t[:, g, 0:P], k_t[:, g, P:2 * P],
                                     start=True, stop=True)
                for g in range(NG):
                    dst = bank[3][:, g * S:(g + 1) * S] if g < 2 else bank[4][:, 0:S]
                    mm = nc.tensor.matmul(dst, q_t[:, g, P:2 * P], k_t[:, g, :], start=True, stop=True)
                mm.then_inc(scores_done, 1)

            def turn_v(h):
                for g in range(NG):
                    for t in range(TT):
                        at = (g % 2) * S + t * P
                        mm = nc.tensor.transpose(bank[5 + g // 2][:, at:at + P], v_t[:, g, t * P:(t + 1) * P],
                                                 ident[:, :])
                mm.then_inc(v_turned, 1)

            def turn_probs(h):
                pe.wait_ge(prob_ready, 2 * (h + 1))
                for g in range(NG):
                    late = NG * P + g * S
                    for n, col in enumerate((g * P, late + P, late)):
                        mm = nc.tensor.transpose(bank[2 + g][:, n * P:(n + 1) * P], prob[:, col:col + P], ident[:, :])
                mm.then_inc(prob_turned, 1)

            def attend(h):
                pe.wait_ge(prob_copied, NG * (h + 1))
                pe.wait_ge(v_copied, 2 * (h + 1))
                for g in range(NG):
                    nc.tensor.matmul(bank[7][:, 0:S], v_rows[:, g, 1, :], prob_t[:, g, 0:S], start=(g == 0), stop=False)
                for g in range(NG):
                    mm = nc.tensor.matmul(bank[7][:, P:S], v_rows[:, g, 0, :], prob_t[:, g, S:S + P],
                                          start=False, stop=(g == NG - 1))
                mm.then_inc(attended, 1)

            def head_slab_product(h, j, ready=None):
                if isinstance(h, int) and h == 0 and j < 2:
                    pe.wait_ge(qb_lo, 2 * (j + 1))
                else:
                    pe.wait_ge(summed, 3 * KT + h * QKV.per_turn + (j - 1))
                project(pe, QKV, h, j, bank[j % 2], act_a if j < 2 * NG else act_b, ready)

            for j in range(QKV.per_turn):
                head_slab_product(0, j, {0: kv_lo, 2 * NG: qb_lo}.get(j))
            with pe.Fori(1, HEADS) as h:
                for j in range(QKV.per_turn):
                    head_slab_product(h, j)
                    if j == 0:
                        scores(h - 1)
                        turn_v(h - 1)
                    if j == 3:
                        turn_probs(h - 1)
                    if j == 6:
                        attend(h - 1)

            last = HEADS - 1
            for c in range(CHUNKS):
                if c >= 2:
                    pe.wait_ge(x2_added, TT * (c - 1))
                if c == 1:
                    pe.wait_ge(prob_copied, NG * HEADS)
                if c == 0:
                    pe.wait_ge(summed, 3 * KT + HEADS * QKV.per_turn)
                    scores(last)
                    turn_v(last)
                for q in range(B_OUT.per_turn - (c == CHUNKS - 1)):
                    out_project(pe, B_OUT, c, q, bank[2 * (c % 2):2 * (c % 2) + 2], act_a, y2_lo if c == 0 else None)
                    if c == 0 and q == 1:
                        turn_probs(last)
                    if c == 0 and q == 2:
                        attend(last)
            out_project_last(pe, B_OUT, bank[2:4], act_a, b_first_done)


INPUTS = ["x", "a_norm", "a_w_in", "a_conv_w", "a_conv_b", "a_ln_g", "a_ln_b", "a_w_out", "kv_norm", "w_kv",
          "b_norm", "b_w_in", "b_w_out", "rel_bias", "final_norm"]


def bucket_table():
    table = np.zeros((BUCKETS + 1, NG, BIAS_W), np.float32)
    exact = BUCKETS // 2
    for g, (window, dil) in enumerate(GROUPS):
        for e in range(BIAS_W):
            dist = e - (S - 1)
            if dist < 0 or dist % dil or dist > window:
                table[BUCKETS, g, e] = 1.0
                continue
            bucket = dist
            if dist >= exact:
                bucket = exact + int(math.log(dist / exact) / math.log(MAX_DISTANCE / exact) * (BUCKETS - exact))
            table[min(bucket, BUCKETS - 1), g, e] = 1.0
    return table.reshape(BUCKETS + 1, NG * BIAS_W)


def kernel(**inputs):
    import concourse.bacc as bacc
    from concourse.bass_utils import run_bass_kernel_spmd

    nc = bacc.Bacc("TRN2", target_bir_lowering=False, num_devices=1)
    arrays = {name: np.ascontiguousarray(inputs[name]) for name in INPUTS}
    arrays["bucket_rows"] = bucket_table()
    args = [nc.dram_tensor(f"{n}_dram", a.shape, mybir.dt.from_np(a.dtype), kind="ExternalInput").ap()
            for n, a in arrays.items()]
    out = nc.dram_tensor("out_dram", (1, S, D), F32, kind="ExternalOutput").ap()
    build(nc, *args, out)
    done = run_bass_kernel_spmd(nc, [{f"{n}_dram": a for n, a in arrays.items()}], core_ids=[0])
    return done.results[0]["out_dram"]
```
